# Optimizing a Trainium2 kernel written in Bass

```python
import math
import jax, jax.numpy as jnp
from jax import lax
import numpy as np

D_MODEL = 1024
BATCH = 1
SEQ = 2048
DEPTH = 1
DEC_BATCH = 8
DEC_SEQ = 1
PAST_LEN = 16384
PAGE_SIZE = 128

MIX_DIM = D_MODEL
CONV_DIM = MIX_DIM // 2
CONV_W = 3
MLSTM_DIM = MIX_DIM - CONV_DIM
MLSTM_HEADS = 4
MLSTM_DQK = MLSTM_DIM // MLSTM_HEADS
MLSTM_DV = MLSTM_DIM // MLSTM_HEADS
MLSTM_CHUNK = 64
N_MEM = 256
X_HEADS = 4
X_HEAD_DIM = D_MODEL // X_HEADS
D_FF = -(-8 * D_MODEL // (3 * 256)) * 256
IN_DIM = 3 * CONV_DIM + 4 * MLSTM_DIM + 2 * MLSTM_HEADS
EPS = 1e-6

kernel_name = 'hymba_conv_mlstm_memxattn_step'

def rmsnorm(x, g):
    x32 = x.astype(jnp.float32)
    y = x32 * lax.rsqrt(jnp.mean(x32 * x32, axis=-1, keepdims=True) + EPS) * g.astype(jnp.float32)
    return y.astype(x.dtype)

def short_conv(u, conv_state, conv_w):
    T = u.shape[1]
    up = jnp.concatenate([conv_state.astype(u.dtype), u], axis=1)
    y = conv_w[0] * up[:, 0:T]
    for j in range(1, CONV_W):
        y = y + conv_w[j] * up[:, j:j + T]
    return y, up[:, T:]

def mlstm_chunk(carry, inp):
    C, n, m = carry
    q, k, v, ig, lf = inp
    L = q.shape[2]
    b = jnp.cumsum(lf, axis=-1)
    causal = jnp.tril(jnp.ones((L, L), dtype=bool))
    dmat = jnp.where(causal, b[..., :, None] - b[..., None, :] + ig[..., None, :], -jnp.inf)
    inter = b + m[..., None]
    m_row = jnp.maximum(inter, jnp.max(dmat, axis=-1))
    w = jnp.einsum('bhld,bhsd->bhls', q, k) * jnp.exp(dmat - m_row[..., None])
    g = jnp.exp(inter - m_row)
    num = g[..., None] * jnp.einsum('bhvd,bhld->bhlv', C, q) + jnp.einsum('bhls,bhsv->bhlv', w, v)
    den = g * jnp.einsum('bhd,bhld->bhl', n, q) + jnp.sum(w, axis=-1)
    h = num / jnp.maximum(jnp.abs(den), jnp.exp(-m_row))[..., None]
    b_last = b[..., -1]
    a = b_last[..., None] - b + ig
    m_new = jnp.maximum(b_last + m, jnp.max(a, axis=-1))
    decay = jnp.exp(b_last + m - m_new)
    s = jnp.exp(a - m_new[..., None])
    C_new = decay[..., None, None] * C + jnp.einsum('bhs,bhsv,bhsd->bhvd', s, v, k)
    n_new = decay[..., None] * n + jnp.einsum('bhs,bhsd->bhd', s, k)
    return (C_new, n_new, m_new), h

def mlstm(q, k, v, ig, lf, C0, n0, m0, chunk):
    B, T = q.shape[0], q.shape[1]
    nc = T // chunk

    def to_chunks(a):
        a = a.reshape((B, nc, chunk) + a.shape[2:])
        return jnp.moveaxis(jnp.moveaxis(a, 1, 0), 2, 3)

    carry, h = lax.scan(mlstm_chunk, (C0, n0, m0),
                        (to_chunks(q), to_chunks(k), to_chunks(v), to_chunks(ig), to_chunks(lf)))
    h = jnp.moveaxis(jnp.moveaxis(h, 3, 2), 0, 1).reshape(B, T, MLSTM_HEADS, MLSTM_DV)
    return h, carry

def hybrid_mixer(xn, conv_state, C0, n0, m0, w_in, b_in, conv_w, g_mh, w_out, chunk):
    B, T, _ = xn.shape
    dt = xn.dtype
    proj = xn @ w_in + b_in
    splits = np.cumsum([CONV_DIM] * 3 + [MLSTM_DIM] * 4).tolist()
    gb, gc, hc, q, k, v, o, gates = jnp.split(proj, splits, axis=-1)
    y_conv, new_conv = short_conv(gc * hc, conv_state, conv_w)
    y_conv = gb * y_conv
    f32 = jnp.float32
    qh = q.reshape(B, T, MLSTM_HEADS, MLSTM_DQK).astype(f32)
    kh = k.reshape(B, T, MLSTM_HEADS, MLSTM_DQK).astype(f32) * (MLSTM_DQK ** -0.5)
    vh = v.reshape(B, T, MLSTM_HEADS, MLSTM_DV).astype(f32)
    ig = gates[..., :MLSTM_HEADS].astype(f32)
    lf = jax.nn.log_sigmoid(gates[..., MLSTM_HEADS:].astype(f32))
    h, (C, n, m) = mlstm(qh, kh, vh, ig, lf, C0.astype(f32), n0.astype(f32), m0.astype(f32), chunk)
    h = h * lax.rsqrt(jnp.mean(h * h, axis=-1, keepdims=True) + EPS)
    h = (h.reshape(B, T, MLSTM_DIM) * g_mh.astype(f32)).astype(dt)
    y_ml = jax.nn.sigmoid(o) * h
    out = jnp.concatenate([y_conv, y_ml], axis=-1) @ w_out
    return out, new_conv, C.astype(C0.dtype), n.astype(n0.dtype), m.astype(m0.dtype)

def mem_kv(mem, g_mem, w_xkv):
    B, M, _ = mem.shape
    kk, vv = jnp.split(rmsnorm(mem, g_mem) @ w_xkv, 2, axis=-1)
    return kk.reshape(B, M, X_HEADS, X_HEAD_DIM), vv.reshape(B, M, X_HEADS, X_HEAD_DIM)

def cross_attn(xn, mk, mv, w_xq, w_xo):
    B, T, _ = xn.shape
    q = (xn @ w_xq).reshape(B, T, X_HEADS, X_HEAD_DIM)
    s = jnp.einsum('bthd,bmhd->bhtm', q, mk.astype(q.dtype)).astype(jnp.float32) * (X_HEAD_DIM ** -0.5)
    p = jax.nn.softmax(s, axis=-1).astype(xn.dtype)
    o = jnp.einsum('bhtm,bmhd->bthd', p, mv.astype(xn.dtype)).reshape(B, T, X_HEADS * X_HEAD_DIM)
    return o @ w_xo

def swiglu(xn, w_gu, w_down):
    g, u = jnp.split(xn @ w_gu, 2, axis=-1)
    return (jax.nn.silu(g) * u) @ w_down

def setup_inputs(seed: int = 0) -> dict:
    key = jax.random.key(seed)
    ks = jax.random.split(key, 32)
    nrm = jax.random.normal
    f = jnp.float32
    b_in = 0.02 * nrm(ks[10], (DEPTH, IN_DIM), f)
    b_in = b_in.at[:, -MLSTM_HEADS:].add(jnp.linspace(3.0, 6.0, MLSTM_HEADS, dtype=f))
    return {
        'x_prompt': nrm(ks[0], (BATCH, SEQ, D_MODEL), f),
        'x_sample': nrm(ks[1], (DEC_BATCH, DEC_SEQ, D_MODEL), f),
        'mem_prompt': nrm(ks[2], (BATCH, N_MEM, D_MODEL), f),
        'state_conv': nrm(ks[3], (DEPTH, DEC_BATCH, CONV_W - 1, CONV_DIM), f),
        'state_mlstm_C': 0.3 * nrm(ks[4], (DEPTH, DEC_BATCH, MLSTM_HEADS, MLSTM_DV, MLSTM_DQK), f),
        'state_mlstm_n': 0.3 * nrm(ks[5], (DEPTH, DEC_BATCH, MLSTM_HEADS, MLSTM_DQK), f),
        'state_mlstm_m': nrm(ks[6], (DEPTH, DEC_BATCH, MLSTM_HEADS), f),
        'cache_mem_k': nrm(ks[7], (DEPTH, DEC_BATCH, N_MEM, X_HEADS, X_HEAD_DIM), f),
        'cache_mem_v': nrm(ks[8], (DEPTH, DEC_BATCH, N_MEM, X_HEADS, X_HEAD_DIM), f),
        'g_mix': 1.0 + 0.02 * nrm(ks[9], (DEPTH, D_MODEL), f),
        'w_in': nrm(ks[11], (DEPTH, D_MODEL, IN_DIM), f) * D_MODEL ** -0.5,
        'b_in': b_in,
        'conv_w': nrm(ks[12], (DEPTH, CONV_W, CONV_DIM), f) * CONV_W ** -0.5,
        'g_mh': 1.0 + 0.02 * nrm(ks[13], (DEPTH, MLSTM_DIM), f),
        'w_out': nrm(ks[14], (DEPTH, MIX_DIM, D_MODEL), f) * MIX_DIM ** -0.5,
        'g_cross': 1.0 + 0.02 * nrm(ks[15], (DEPTH, D_MODEL), f),
        'g_mem': 1.0 + 0.02 * nrm(ks[16], (DEPTH, D_MODEL), f),
        'w_xq': nrm(ks[17], (DEPTH, D_MODEL, X_HEADS * X_HEAD_DIM), f) * D_MODEL ** -0.5,
        'w_xkv': nrm(ks[18], (DEPTH, D_MODEL, 2 * X_HEADS * X_HEAD_DIM), f) * D_MODEL ** -0.5,
        'w_xo': nrm(ks[19], (DEPTH, X_HEADS * X_HEAD_DIM, D_MODEL), f) * (X_HEADS * X_HEAD_DIM) ** -0.5,
        'g_ffn': 1.0 + 0.02 * nrm(ks[20], (DEPTH, D_MODEL), f),
        'w_gu': nrm(ks[21], (DEPTH, D_MODEL, 2 * D_FF), f) * D_MODEL ** -0.5,
        'w_down': nrm(ks[22], (DEPTH, D_FF, D_MODEL), f) * D_FF ** -0.5,
        'g_final': 1.0 + 0.02 * nrm(ks[23], (D_MODEL,), f),
    }

def reference(x_prompt, x_sample, mem_prompt, state_conv, state_mlstm_C, state_mlstm_n, state_mlstm_m,
              cache_mem_k, cache_mem_v, g_mix, w_in, b_in, conv_w, g_mh, w_out, g_cross, g_mem,
              w_xq, w_xkv, w_xo, g_ffn, w_gu, w_down, g_final):
    Bp, Tp = x_prompt.shape[0], x_prompt.shape[1]
    dt = x_prompt.dtype
    chunk_p = math.gcd(Tp, MLSTM_CHUNK)
    chunk_s = x_sample.shape[1]
    hp, hs = x_prompt, x_sample
    pcv, pCs, pns, pms, pks, pvs = [], [], [], [], [], []
    scv, sCs, sns, sms = [], [], [], []
    for l in range(DEPTH):
        zc = jnp.zeros((Bp, CONV_W - 1, CONV_DIM), dt)
        zC = jnp.zeros((Bp, MLSTM_HEADS, MLSTM_DV, MLSTM_DQK), dt)
        zn = jnp.zeros((Bp, MLSTM_HEADS, MLSTM_DQK), dt)
        zm = jnp.zeros((Bp, MLSTM_HEADS), dt)
        mp, pc, pC, pn, pm = hybrid_mixer(rmsnorm(hp, g_mix[l]), zc, zC, zn, zm, w_in[l], b_in[l],
                                          conv_w[l], g_mh[l], w_out[l], chunk_p)
        ms, sc, sC, sn, sm = hybrid_mixer(rmsnorm(hs, g_mix[l]), state_conv[l], state_mlstm_C[l],
                                          state_mlstm_n[l], state_mlstm_m[l], w_in[l], b_in[l],
                                          conv_w[l], g_mh[l], w_out[l], chunk_s)
        hp = hp + mp
        hs = hs + ms
        pk, pv = mem_kv(mem_prompt, g_mem[l], w_xkv[l])
        hp = hp + cross_attn(rmsnorm(hp, g_cross[l]), pk, pv, w_xq[l], w_xo[l])
        hs = hs + cross_attn(rmsnorm(hs, g_cross[l]), cache_mem_k[l], cache_mem_v[l], w_xq[l], w_xo[l])
        hp = hp + swiglu(rmsnorm(hp, g_ffn[l]), w_gu[l], w_down[l])
        hs = hs + swiglu(rmsnorm(hs, g_ffn[l]), w_gu[l], w_down[l])
        pcv.append(pc); pCs.append(pC); pns.append(pn); pms.append(pm); pks.append(pk); pvs.append(pv)
        scv.append(sc); sCs.append(sC); sns.append(sn); sms.append(sm)
    y_prompt = rmsnorm(hp, g_final)
    y_sample = rmsnorm(hs, g_final)
    p_conv, p_C, p_n, p_m = jnp.stack(pcv), jnp.stack(pCs), jnp.stack(pns), jnp.stack(pms)
    p_mem_k, p_mem_v = jnp.stack(pks), jnp.stack(pvs)
    s_conv, s_C, s_n, s_m = jnp.stack(scv), jnp.stack(sCs), jnp.stack(sns), jnp.stack(sms)
    return (y_prompt, y_sample, p_conv, p_C, p_n, p_m, p_mem_k, p_mem_v, s_conv, s_C, s_n, s_m)


_drawn_inputs = setup_inputs


def setup_inputs(seed=0):
    import zlib

    import numpy as np

    out = dict(_drawn_inputs(seed))
    spreads = {}
    factors = {'g_mh': 8.0, 'g_cross': 8.0, 'g_mem': 2.854, 'g_ffn': 4.813, 'g_final': 2.893}
    for name, (base, spread) in spreads.items():
        noise = np.random.default_rng([zlib.crc32(name.encode()), seed]).standard_normal(out[name].shape)
        drawn = base * np.exp(spread * noise) if base else spread * noise
        out[name] = __import__('jax').numpy.asarray(drawn.astype(out[name].dtype))
    for name, factor in factors.items():
        out[name] = (out[name] * factor).astype(out[name].dtype)
    return out
```

```python
from contextlib import ExitStack

import numpy as np
import concourse.bass as bass
from concourse import mybir

F32 = mybir.dt.float32
F32R = mybir.dt.float32r
ALU = mybir.AluOpType
ACT = mybir.ActivationFunctionType
AX = mybir.AxisListType

P = 128
D = 1024
KT = D // P
SEQ = 2048
NDEC = 8
BLOCKS = 4
TOK = SEQ // BLOCKS
DEC = NDEC // BLOCKS
W = TOK + DEC
GROUPS = [(0, 258), (258, W - 258)]
HEADS = 4
NMEM = 256
MT = NMEM // P
CHUNK = 128
CH = TOK // CHUNK
FF = 2816
FFG = [8, 7, 7]
EPS = 1e-6
KSCALE = P ** -0.5
XSCALE = 256 ** -0.5
MASKED = -1e30

G_KV = 16
O_GATE = 0
O_HEAD = 2
PER_HEAD = 7
O_OUT = O_HEAD + HEADS * PER_HEAD
O_XQ = O_OUT + KT
O_XO = O_XQ + KT
O_FF = []
_o = O_XO + KT
for _n in FFG:
    O_FF.append(_o)
    _o += 2 * _n + KT
G_BLK = _o
G_ALL = G_KV + BLOCKS * G_BLK

C_BIN = 0
C_BK = 32
C_GI, C_GF = 36, 37
C_CW = 38
C_GMH = 50
C_GMIX, C_GCROSS, C_GMEM, C_GFFN, C_GFIN = 54, 62, 70, 78, 86
C_EPS = 94
NCST = 96

STEPS = {"v_gate": 14, "v_head": 26, "v_att": 26}


class Steps:

    def __init__(self, eng, sem, base, name, per):
        self.eng, self.sem, self.base, self.n, self.name, self.per = eng, sem, base, 0, name, per

    def __call__(self, ins):
        ins.then_inc(self.sem, 1)
        self.n += 1

    def settle(self):
        self.eng.wait_ge(self.sem, self.base + self.n)

    def end(self):
        if self.per != self.n:
            raise ValueError(f"{self.name}: {self.n} steps, declared {self.per}")


class Gemm:

    def __init__(self, half, k=0):
        self.half, self.k = half + k // 2, k % 2

    def at(self, k):
        return Gemm(self.half, self.k + k)

    @property
    def slot(self):
        return self.k

    @property
    def twice(self):
        return self.half * 4 + 2 * self.k


def trunk(nc, x_blk, mem_x, w_kv, w_st, cst_d, mats_d, st_conv, st_c, st_n, st_m, kvc_d,
          y, o_pconv, o_pc, o_pm, o_mk, o_mv, o_sconv, o_sc, o_sn, o_sm, rows_d):
    with ExitStack() as ctx:
        def sb(name, shape, dt=F32):
            return ctx.enter_context(nc.sbuf_tensor(name, shape, dt))

        def sem(name):
            return ctx.enter_context(nc.semaphore(name))

        def one(ap):
            return ap.rearrange("o p c -> (o p) c")

        x = sb("x", [P, KT, W])
        xn_hi = sb("xn_hi", [P, KT, W], F32R)
        xn_lo = sb("xn_lo", [P, KT, W], F32R)
        act_hi = sb("act_hi", [P, KT, W], F32R)
        act_lo = sb("act_lo", [P, KT, W], F32R)
        w_raw = sb("w_raw", [P, 2, D])
        w_hi = sb("w_hi", [P, 2, D], F32R)
        w_lo = sb("w_lo", [P, 2, D], F32R)
        mem_kt = sb("mem_kt", [P, KT, NMEM])
        mem_v = sb("mem_v", [P, MT, D])
        big = sb("big", [P, 8232])
        work = sb("work", [P, 6664])
        state = sb("state", [P, HEADS, 256])
        r_mix = sb("r_mix", [P, W])
        r_res = sb("r_res", [P, W])
        acc_mix = sb("acc_mix", [P, W])
        acc_res = sb("acc_res", [P, W])
        sq_mix = sb("sq_mix", [P, W])
        sq_res = sb("sq_res", [P, W])
        lnt = sb("lnt", [P, W])
        cst = sb("cst", [P, NCST])
        mats = sb("mats", [P, 3 * P + W])
        ident, ones, maskneg = (mats[:, i * P:(i + 1) * P] for i in range(3))
        reset = mats[:, 3 * P:3 * P + W]
        a_row = sb("a_row", [P, W])
        carry = sb("carry", [P, HEADS, 2])
        m_st = sb("m_st", [P, CH + 1])
        d0 = sb("d0", [P, TOK])
        m_dec = sb("m_dec", [P, DEC])
        m_deco = sb("m_deco", [P, DEC])
        cv_in = sb("cv_in", [P, HEADS, 2, DEC])
        cv_out = sb("cv_out", [P, HEADS, 2, DEC])

        cursor = {"big": 0, "work": 0}

        def cut(which, n, reset_to=None):
            if reset_to is not None:
                cursor[which] = reset_to
            a = cursor[which]
            cursor[which] = a + n
            t = big if which == "big" else work
            return t[:, a:a + n]

        qf, kf, vf, of = (cut("big", W) for _ in range(4))
        qg = cut("big", W)
        emat = cut("big", TOK)
        numden = cut("big", 2 * W).rearrange("p (a c) -> p a c", a=2)
        cgb, cgc, chc = (cut("big", W) for _ in range(3))
        ub = cut("big", W + 2)
        yc = cut("big", W)
        bc = cut("big", 3 * W + DEC)
        rows = bc
        gi, gz, gt1, brow = cgb, cgc, chc, yc
        ktv = cut("work", 2 * 384).rearrange("p (s c) -> p s c", s=2)
        w_sb = cut("work", 2 * P).rearrange("p (s c) -> p s c", s=2)
        vs_sb = cut("work", 2 * 256).rearrange("p (s c) -> p s c", s=2)
        ws = cut("work", 256)
        ds_dec = cut("work", DEC * 256).rearrange("p (s c) -> p s c", s=DEC)
        dk = cut("work", DEC * 384).rearrange("p (s c) -> p s c", s=DEC)
        dvs = cut("work", DEC * 256).rearrange("p (s c) -> p s c", s=DEC)
        a_col = cut("work", CH * HEADS).rearrange("p (c h) -> p c h", c=CH)
        n_dec = cut("work", DEC)
        hraw = cut("work", W)
        hsq = cut("work", W)
        hr = cut("work", W)
        kc = big[:, 0:4096].rearrange("p (i m) -> p i m", m=NMEM)
        vc = big[:, 4096:8192].rearrange("p (i d) -> p i d", d=D)
        q_att = cut("work", 2 * 2 * W, 0).rearrange("p (s t c) -> p s t c", s=2, t=2)
        prob = cut("work", 4 * NMEM).rearrange("p (s m) -> p s m", s=4)
        prob_t = cut("work", MT * TOK).rearrange("p (t c) -> p t c", t=MT)
        mx = cut("work", 16).rearrange("p (s c) -> p s c", s=4)
        qd = cut("work", KT * DEC).rearrange("p (k b) -> p k b", k=KT)
        s_t = cut("work", 16)
        pd = cut("work", NMEM)
        p_t = cut("work", 16)
        dmx = cut("work", 4)
        x_next = big[:, 0:KT * W].rearrange("p (k c) -> p k c", k=KT)
        gt = cut("work", W, 0)
        ut = cut("work", W)
        et = cut("work", W)
        ht = cut("work", W)
        memx = x_next[:, :, 0:NMEM]
        vfeat = big[:, 4112:4112 + 2048].rearrange("p (k m) -> p k m", k=KT)

        gb = ctx.enter_context(nc.psum_tensor("gb", [P, 4, 512], F32))
        ta = ctx.enter_context(nc.psum_tensor("ta", [P, 2, 512], F32))
        tb = ctx.enter_context(nc.psum_tensor("tb", [P, 512], F32))
        td = ctx.enter_context(nc.psum_tensor("td", [P, 512], F32))

        def sems(names):
            return [sem(n) for n in names.split()]

        cst_loaded, memx_loaded, xnext_loaded, x_loaded, set_up = sems(
            "cst_loaded memx_loaded xnext_loaded x_loaded set_up")
        w_loaded = sems("w_loaded_even w_loaded_odd")
        w_hi_done, w_lo_done, group_done, evacuated = sems("w_hi_done w_lo_done group_done evacuated")
        mix_hi, mix_sq, mix_lo, mix_acc = sems("mix_hi mix_sq mix_lo mix_acc")
        res_hi, res_sq, res_lo, res_acc = sems("res_hi res_sq res_lo res_acc")
        ssq_done, ln_done, r_done = sems("ssq_done ln_done r_done")
        v_gate, v_head, v_att, v_dec, v_ffn = sems("v_gate v_head v_att v_dec v_ffn")
        a_gate, a_head = sems("a_gate a_head")
        gate_i, ls_done, rows_pre, rows_exp, rows_stored = sems("gate_i ls_done rows_pre rows_exp rows_stored")
        bc_loaded, bc_used, c_loaded, n_loaded, st_stored = sems("bc_loaded bc_used c_loaded n_loaded st_stored")
        bias_done, acol_t, acol_done, e_pre, e_done = sems("bias_done acol_t acol_done e_pre e_done")
        t_done, ktv_done, w_done, vs_done, qg_done = sems("t_done ktv_done w_done vs_done qg_done")
        n_done, nd_evac, state_done = sems("n_done nd_evac state_done")
        td_done, dk_done, dvs_done, dupd_done, dstate_done, dn_done, dnd_evac = sems(
            "td_done dk_done dvs_done dupd_done dstate_done dn_done dnd_evac")
        h_done, hsq_done, hn_done, hr_done, a_sig, sig_pre, sig_done = sems("h_done hsq_done hn_done hr_done a_sig sig_pre sig_done")
        conv_bias, yc_done, yh_done, y_hi, y_lo = sems("conv_bias yc_done yh_done y_hi y_lo")
        cache_loaded, s_done, mx_done, exp_done, p_done, pt_done, pt_evac = sems(
            "cache_loaded s_done mx_done exp_done p_done pt_done pt_evac")
        pv_done, o_hi, o_lo, qd_done, do_hi, do_lo = sems("pv_done o_hi o_lo qd_done do_hi do_lo")
        ds_done, ds_evac, dst_done, dmx_done, dexp_done, dp_done, dpt_done, dpt_evac, dpv_done = sems(
            "ds_done ds_evac dst_done dmx_done dexp_done dp_done dpt_done dpt_evac dpv_done")
        dp_seen = sem("dp_seen")
        e_ffn, h_ffn, hid_hi, hid_lo = sems("e_ffn h_ffn hid_hi hid_lo")
        y_ready, y_stored, out_stored, vt_done, vt_evac, kv_stored = sems(
            "y_ready y_stored out_stored vt_done vt_evac kv_stored")
        m_stored, mdec_loaded, cvin_loaded, cv_stored = sems("m_stored mdec_loaded cvin_loaded cv_stored")

        def g_head(b, j, u):
            return Gemm(b * (G_BLK // 2) + j * PER_HEAD + (G_KV + O_HEAD) // 2, u * PER_HEAD)

        def g_blk(b, off, j=0):
            return Gemm(b * (G_BLK // 2) + j + (G_KV + off) // 2)

        def read_out(eng, g):
            eng.wait_ge(evacuated, g.twice + 6)

        def tile(t, e, n=1):
            return t[:, bass.ds(e, 1), :].rearrange("p o c -> p (o c)")

        def cols(t, e, n):
            c, wd = GROUPS[n]
            return t[:, bass.ds(e, 1), c:c + wd].rearrange("p o c -> p (o c)")

        block = ctx.enter_context(nc.Block())

        @block.sync
        def _(sp):
            sp.dma_start(memx, mem_x.rearrange("p (k c) -> p k c", k=KT)).then_inc(memx_loaded, 16)
            sp.dma_start(cst[:], cst_d).then_inc(cst_loaded, 16)
            sp.dma_start(mats[:], mats_d).then_inc(cst_loaded, 16)
            for i in range(2):
                sp.dma_start(w_raw[:, i, :], w_kv[i]).then_inc(w_loaded[i], 16)
            with sp.Fori(1, G_KV // 2, 1) as j:
                for i in range(2):
                    sp.wait_ge(w_lo_done, j * 2 + i - 1)
                    sp.dma_start(w_raw[:, i, :], one(w_kv[bass.ds(j * 2 + i, 1)])).then_inc(w_loaded[i], 16)
            with sp.Fori(0, BLOCKS, 1) as b:
                with sp.Fori(0, G_BLK // 2, 1) as j:
                    for i in range(2):
                        sp.wait_ge(w_lo_done, b * G_BLK + j * 2 + (G_KV + i - 1))
                        sp.dma_start(w_raw[:, i, :], one(w_st[bass.ds(j * 2 + i, 1)])).then_inc(w_loaded[i], 16)
            for i in range(2):
                sp.wait_ge(w_lo_done, G_ALL + i - 1)
                sp.dma_start(w_raw[:, i, :], w_kv[i]).then_inc(w_loaded[i], 16)

        @block.gpsimd
        def _(pool):
            with pool.Fori(0, G_ALL // 2 + 1, 1) as j:
                for i in range(2):
                    pool.wait_ge(w_hi_done, j * 2 + i + 1)
                    pool.tensor_tensor(w_lo[:, i, :], w_raw[:, i, :], w_hi[:, i, :].bitcast(F32),
                                       ALU.subtract).then_inc(w_lo_done, 1)

        @block.tensor
        def _(pe):
            def group(g, n, col, wd, hi, lo, ks, kwait=None, inc=1, first=True, last=True):
                s = g.slot
                if first:
                    pe.wait_ge(evacuated, g.twice + n + inc)
                for k in ks:
                    if kwait is not None:
                        kwait(k, n)
                    for i, (a, r) in enumerate([(w_hi, hi), (w_hi, lo), (w_lo, hi)]):
                        mm = pe.matmul(gb[:, 2 * s + n, 0:wd], a[:, s, k * P:(k + 1) * P],
                                       r[:, k, col:col + wd], start=(first and k == ks[0] and i == 0),
                                       stop=(last and k == ks[-1] and i == 2))
                if last:
                    mm.then_inc(group_done, inc)

            def gemm(g, hi, lo, kts=KT, kwait=None, after=(None, None), late=()):
                pe.wait_ge(w_lo_done, g.half * 2 + g.k + 1)
                early = [k for k in range(kts) if k not in late]
                for ks in (early, late) if late else (early,):
                    for n, (col, wd) in enumerate(GROUPS):
                        group(g, n, col, wd, hi, lo, ks, kwait, first=ks is early, last=ks is late or not late)
                        if after[n]:
                            after[n]()

            def sumsq(acc, banks, width=W):
                parts = GROUPS if width == W else [(0, width)]
                for bank, (col, wd) in zip(banks, parts):
                    mm = pe.matmul(bank[:, 0:wd], ones, acc[:, col:col + wd], start=True, stop=True)
                mm.then_inc(ssq_done, 1)

            pe.wait_ge(cst_loaded, 32)
            pe.wait_ge(mix_acc, 9)
            sumsq(acc_mix, (td, tb), NMEM)
            for base in (0, KT // 2):
                with pe.Fori(0, KT // 2, 1) as j:
                    for i in range(2):
                        g = Gemm(j + base, i)
                        pe.wait_ge(w_lo_done, g.half * 2 + g.k + 1)
                        group(g, 0, 0, NMEM, xn_hi, xn_lo, range(KT),
                              kwait=lambda k, n: pe.wait_ge(mix_lo, k + 1), inc=2)
            pe.wait_ge(evacuated, 2 * G_KV + 4)
            for q in range(4):
                if q >= 2:
                    pe.wait_ge(vt_evac, q - 1)
                for mt in range(MT):
                    for i in range(2):
                        t = pe.transpose(ta[:, q % 2, mt * 256 + i * P:mt * 256 + (i + 1) * P],
                                         vfeat[:, 2 * q + i, mt * P:(mt + 1) * P], ident)
                t.then_inc(vt_done, 1)
            pe.wait_ge(vt_evac, 4)

            with pe.Fori(0, BLOCKS, 1) as b:
                pe.wait_ge(mix_acc, b * 9 + 18)
                sumsq(acc_mix, (td, tb))
                for i in range(2):
                    gemm(g_blk(b, O_GATE).at(i), xn_hi, xn_lo,
                         kwait=lambda k, n: n or pe.wait_ge(mix_lo, b * 8 + (8 + k + 1)))
                with pe.Fori(0, 2, 1) as j:
                    for u in range(2):
                        hd = b * 4 + j * 2 + u

                        def acols():
                            pe.wait_ge(rows_pre, b + 1)
                            pe.wait_ge(hr_done, hd + 1)
                            for c in range(CH):
                                t = pe.transpose(td[:, c * P:(c + 1) * P], a_row[:, c * P:(c + 1) * P], ident)
                            t.then_inc(acol_t, 1)

                        def t_part(c):
                            bank = ta[:, c % 2, :]
                            if c == 0:
                                pe.wait_ge(bias_done, hd * 3 + 3)
                            if c >= 2:
                                pe.wait_ge(ktv_done, hd * CH + (c - 1))
                                pe.wait_ge(w_done, hd * CH + (c - 1))
                            sl = slice(c * P, (c + 1) * P)
                            pe.transpose(bank[:, 0:P], kf[:, sl], ident)
                            pe.transpose(bank[:, P:2 * P], vf[:, sl], ident)
                            pe.matmul(bank[:, 2 * P:3 * P], kf[:, sl], qf[:, sl],
                                      start=True, stop=True).then_inc(t_done, 1)

                        def n_part(c):
                            sl = slice(c * P, (c + 1) * P)
                            s = c % 2
                            pe.wait_ge(ktv_done, hd * CH + (c + 1))
                            pe.wait_ge(w_done, hd * CH + (c + 1))
                            pe.wait_ge(vs_done, hd * CH + (c + 1))
                            if c == 0:
                                pe.wait_ge(qg_done, hd + 1)
                            else:
                                pe.wait_ge(nd_evac, hd * CH + c)
                            pe.wait_ge(state_done, hd * 5 + (c + 1))
                            pe.matmul(tb[:, 0:P], ws[:, 0:P], qg[:, sl], start=True, stop=False)
                            pe.matmul(tb[:, 0:P], ktv[:, s, P:2 * P], w_sb[:, s, :], start=False, stop=True)
                            pe.matmul(tb[:, P:2 * P], ws[:, P:2 * P], qg[:, sl], start=True, stop=False)
                            pe.matmul(tb[:, P:2 * P], ones, w_sb[:, s, :], start=False, stop=True)
                            pe.matmul(tb[:, 2 * P:4 * P], ktv[:, s, 0:P], vs_sb[:, s, :],
                                      start=True, stop=True).then_inc(n_done, 1)

                        def tdec():
                            pe.wait_ge(ktv_done, hd * CH + 3)
                            pe.wait_ge(w_done, hd * CH + 3)
                            for i in range(DEC):
                                pe.transpose(ta[0:1, 0, i * 256:i * 256 + P], kf[:, TOK + i:TOK + i + 1], ident)
                                t = pe.transpose(ta[0:1, 0, i * 256 + P:i * 256 + 2 * P],
                                                 vf[:, TOK + i:TOK + i + 1], ident)
                            t.then_inc(td_done, 1)

                        def dupd():
                            pe.wait_ge(dvs_done, hd + 1)
                            pe.wait_ge(acol_done, hd + 1)
                            for i in range(DEC):
                                mm = pe.matmul(td[:, i * 256:(i + 1) * 256], dk[0:1, i, 0:P], dvs[0:1, i, :],
                                               start=True, stop=True)
                            mm.then_inc(dupd_done, 1)

                        def dnum():
                            pe.wait_ge(dstate_done, hd + 1)
                            pe.wait_ge(state_done, hd * 5 + 5)
                            for i in range(DEC):
                                q1 = qf[:, TOK + i:TOK + i + 1]
                                pe.matmul(tb[:, i:i + 1], ds_dec[:, i, 0:P], q1, start=True, stop=True)
                                mm = pe.matmul(tb[:, DEC + i:DEC + i + 1], ds_dec[:, i, P:2 * P], q1,
                                               start=True, stop=True)
                            mm.then_inc(dn_done, 1)

                        def hnorm():
                            pe.wait_ge(hsq_done, hd * 2 + 2)
                            pe.wait_ge(dnd_evac, hd + 1)
                            pe.matmul(td[:, 0:GROUPS[0][1]], ones, hsq[:, 0:GROUPS[0][1]], start=True, stop=True)
                            pe.matmul(tb[:, 0:GROUPS[1][1]], ones, hsq[:, GROUPS[1][0]:W],
                                      start=True, stop=True).then_inc(hn_done, 1)

                        g = g_head(b, j, u)
                        for i in range(3):
                            gemm(g.at(i), xn_hi, xn_lo)
                        gemm(g.at(3), xn_hi, xn_lo,
                             after=(lambda: (acols(), t_part(0)), lambda: t_part(1)))
                        gemm(g.at(4), xn_hi, xn_lo,
                             after=(lambda: (n_part(0), t_part(2)), lambda: (n_part(1), t_part(3))))
                        gemm(g.at(5), xn_hi, xn_lo,
                             after=(lambda: (n_part(2), tdec()), lambda: (n_part(3), dupd())))
                        gemm(g.at(6), xn_hi, xn_lo, after=(dnum, hnorm))

                with pe.Fori(0, KT // 2, 1) as j:
                    for i in range(2):
                        gemm(g_blk(b, O_OUT, j).at(i), act_hi, act_lo, late=() if i else (7, 3),
                             kwait=(lambda k, n: n or pe.wait_ge(y_lo, b * 8 + (2 * (k % 4) + 2 - k // 4)))
                             if i == 0 else None)
                def sum_res(use):
                    for n in range(2):
                        pe.wait_ge(res_acc, b * 51 + (use * 17 + 16 + n))
                        c, wd = GROUPS[n]
                        mm = pe.matmul(ta[:, n, 0:wd], ones, acc_res[:, c:c + wd], start=True, stop=True)
                    mm.then_inc(ssq_done, 1)

                def res_wait(use):
                    return lambda k, n: pe.wait_ge(res_lo, b * 32 + (use * 16 + 2 * k + n + 1))

                def xq(m, after=(None, None)):
                    gemm(g_blk(b, O_XQ).at(m), xn_hi, xn_lo, kwait=None if m else res_wait(0), after=after)

                def scores(h):
                    read_out(pe, g_blk(b, O_XQ).at(2 * h + 1))
                    for t in range(CH):
                        for dt in range(2):
                            mm = pe.matmul(ta[:, t // 2, (t % 2) * 256:(t % 2) * 256 + 256],
                                           q_att[:, h % 2, dt, t * P:(t + 1) * P], mem_kt[:, 2 * h + dt, :],
                                           start=(dt == 0), stop=(dt == 1))
                        if t % 2:
                            mm.then_inc(s_done, 1)

                def ptrans(h, ts):
                    for t in ts:
                        pe.wait_ge(p_done, b * 16 + (h * 4 + t + 1))
                        if t >= 2:
                            pe.wait_ge(pt_evac, b * 16 + (h * 4 + t - 1))
                        else:
                            pe.wait_ge(o_lo, b * 8 + (h * 2 + 1))
                        for mt in range(MT):
                            m = pe.transpose((tb, td)[t % 2][:, mt * P:(mt + 1) * P],
                                             prob[:, t, mt * P:(mt + 1) * P], ident)
                        m.then_inc(pt_done, 1)

                def pv(h):
                    pe.wait_ge(pt_evac, b * 16 + (h * 4 + 4))
                    for dt, bank in enumerate((tb, td)):
                        for mt in range(MT):
                            mm = pe.matmul(bank[:, :], mem_v[:, mt, h * 256 + dt * P:h * 256 + (dt + 1) * P],
                                           prob_t[:, mt, :], start=(mt == 0), stop=(mt == MT - 1))
                        mm.then_inc(pv_done, 1)

                def dec_scores():
                    pe.wait_ge(cache_loaded, b * 128 + 128)
                    pe.wait_ge(qd_done, b * 4 + 4)
                    for mt in range(MT):
                        for i in range(DEC):
                            for h in range(HEADS):
                                c = mt * 8 + i * 4 + h
                                for dt in range(2):
                                    mm = pe.matmul(gb[:, 0, c:c + 1], kc[:, i * 8 + h * 2 + dt, mt * P:(mt + 1) * P],
                                                   qd[:, 2 * h + dt, i:i + 1], start=(dt == 0), stop=(dt == 1))
                    mm.then_inc(ds_done, 1)

                def dec_trans():
                    pe.wait_ge(ds_evac, b + 1)
                    for mt in range(MT):
                        m = pe.transpose(gb[0:8, 1, mt * P:(mt + 1) * P], s_t[:, mt * 8:mt * 8 + 8], ident)
                    m.then_inc(dst_done, 1)

                def dec_ptrans():
                    pe.wait_ge(dp_done, b + 1)
                    pe.sem_inc(dp_seen, 1)
                    for mt in range(MT):
                        m = pe.transpose(gb[:, 2, mt * 8:mt * 8 + 8], pd[0:8, mt * P:(mt + 1) * P], ident[0:8, 0:8])
                    m.then_inc(dpt_done, 1)

                def dec_pv():
                    pe.wait_ge(dpt_evac, b + 1)
                    for h in range(HEADS):
                        for dt in range(2):
                            for i in range(DEC):
                                c = (h * 2 + dt) * DEC + i
                                for mt in range(MT):
                                    mm = pe.matmul(gb[:, 3, c:c + 1],
                                                   vc[:, i * 2 + mt, h * 256 + dt * P:h * 256 + (dt + 1) * P],
                                                   p_t[:, mt * 8 + i * 4 + h:mt * 8 + i * 4 + h + 1],
                                                   start=(mt == 0), stop=(mt == MT - 1))
                    mm.then_inc(dpv_done, 1)

                xq(0, after=(lambda: sum_res(0), None))
                xq(1)
                for h in range(HEADS - 1):
                    xq(2 * h + 2, after=(lambda: scores(h), lambda: ptrans(h, (0, 1))))
                    xq(2 * h + 3, after=(lambda: ptrans(h, (2, 3)), lambda: pv(h)))
                h = HEADS - 1
                scores(h)
                dec_scores()
                ptrans(h, (0, 1))
                dec_trans()
                ptrans(h, (2, 3))
                dec_ptrans()
                pv(h)
                dec_pv()
                with pe.Fori(0, KT // 2, 1) as j:
                    for i in range(2):
                        gemm(g_blk(b, O_XO, j).at(i), act_hi, act_lo,
                             kwait=lambda k, n: n or k or pe.wait_ge(do_lo, b + 1))
                def gu(gr, f, after=(None, None)):
                    g = g_blk(b, O_FF[gr], f)
                    gemm(g.at(0), xn_hi, xn_lo, kwait=None if gr else res_wait(1), after=after)
                    gemm(g.at(1), xn_hi, xn_lo)

                gu(0, 0, after=(lambda: sum_res(1), None))
                fo = 0
                for gr, size in enumerate(FFG):
                    with pe.Fori(0 if gr else 1, size, 1) as f:
                        gu(gr, f)
                    with pe.Fori(0, KT // 2, 1) as j:
                        for i in range(2):
                            gemm(g_blk(b, O_FF[gr] + 2 * size, j).at(i), act_hi, act_lo, kts=size,
                                 kwait=(lambda k, n: pe.wait_ge(hid_lo, b * 44 + (2 * (fo + k) + n + 1)))
                                 if i == 0 else None)
                    fo += size
                sum_res(2)

        @block.scalar
        def _(act):
            act.preload_act_table_set("natural_log_exp_and_others")

            def w_high(g):
                s = g.slot
                act.wait_ge(w_loaded[s], g.half * 16 + 32)
                act.wait_ge(group_done, g.twice + 2)
                act.activation(w_hi[:, s, :], w_raw[:, s, :], ACT.Copy).then_inc(w_hi_done, 1)

            def col(c):
                return cst[:, c:c + 1]

            def dyn(c, e):
                return cst[:, bass.ds(e + c, 1)]

            def rnorm(r, banks, index, width=W):
                act.wait_ge(ssq_done, index + 1)
                parts = GROUPS if width == W else [(0, width)]
                for bank, (c, wd) in zip(banks, parts):
                    a = act.activation(lnt[:, c:c + wd], bank[:, 0:wd], ACT.Ln, scale=1.0 / D, bias=col(C_EPS))
                a.then_inc(ln_done, 1)
                act.wait_ge(ln_done, index + 1)
                act.activation(r[:, 0:width], lnt[:, 0:width], ACT.Exp, scale=-0.5).then_inc(r_done, 1)

            act.wait_ge(cst_loaded, 32)
            act.wait_ge(memx_loaded, 16)
            for k in range(KT):
                act.activation(xn_hi[:, k, 0:NMEM], memx[:, k, :], ACT.Copy, scale=col(C_GMEM + k)).then_inc(mix_hi, 1)
                act.wait_ge(mix_acc, k + 1)
                act.activation(sq_mix[:, 0:NMEM], memx[:, k, :], ACT.Square).then_inc(mix_sq, 1)
            for i in range(2):
                act.wait_ge(w_loaded[i], 16)
                act.activation(w_hi[:, i, :], w_raw[:, i, :], ACT.Copy).then_inc(w_hi_done, 1)
            act.wait_ge(mix_lo, 8)
            act.wait_ge(mix_sq, 8)
            act.dma_start(x_next, x_blk[0:KT].rearrange("k p c -> p k c")).then_inc(xnext_loaded, 16)
            rnorm(r_mix, (td, tb), 0, NMEM)
            for base in (0, KT // 2):
                with act.Fori(0, KT // 2, 1) as j:
                    for i in range(2):
                        w_high(Gemm(j + base, i))
            act.wait_ge(evacuated, 2 * G_KV + 4)
            act.dma_start(o_mk, mem_kt[:].rearrange("p k m -> p (k m)")).then_inc(kv_stored, 16)
            act.dma_start(o_mv, vfeat.rearrange("p k m -> p (k m)")).then_inc(kv_stored, 16)
            for q in range(4):
                act.wait_ge(vt_done, q + 1)
                act.activation(mem_v[:, :, q * 256:(q + 1) * 256],
                               ta[:, q % 2, :].rearrange("p (t d) -> p t d", t=MT), ACT.Copy).then_inc(vt_evac, 1)
            act.wait_ge(xnext_loaded, 16)
            for k in range(KT):
                act.activation(xn_hi[:, k, :], x_next[:, k, :], ACT.Copy, scale=col(C_GMIX + k)).then_inc(mix_hi, 1)
                act.wait_ge(mix_acc, 9 + k + 1)
                act.activation(sq_mix[:], x_next[:, k, :], ACT.Square).then_inc(mix_sq, 1)
            act.wait_ge(kv_stored, 32)

            with act.Fori(0, BLOCKS, 1) as b:
                act.dma_start(m_dec[:], one(st_m[bass.ds(b, 1)])).then_inc(mdec_loaded, 16)
                act.dma_start(cv_in[:].rearrange("p a b c -> p (a b c)"),
                              one(st_conv[bass.ds(b, 1)])).then_inc(cvin_loaded, 16)
                rnorm(r_mix, (td, tb), b * 4 + 1)
                g = g_blk(b, O_GATE)
                w_high(g)
                read_out(act, g)
                act.activation(gi, gi, ACT.Identity, bias=col(C_GI)).then_inc(gate_i, 1)
                w_high(g.at(1))
                read_out(act, g.at(1))
                st = Steps(act, a_gate, b * 3, "a_gate", 3)
                st(act.activation(gz, gz, ACT.Identity, bias=col(C_GF)))
                st.settle()
                st(act.activation(gt1, gz, ACT.Abs))
                st.settle()
                st(act.activation(gt1, gt1, ACT.Exp, scale=-1.0))
                st.settle()
                act.activation(gt1, gt1, ACT.Ln, bias=1.0).then_inc(ls_done, 1)
                st.end()
                act.wait_ge(rows_pre, b + 1)
                act.activation(rows[:, W:2 * W + DEC], rows[:, W:2 * W + DEC], ACT.Exp)
                act.activation(rows[:, 2 * W + DEC:], rows[:, 2 * W + DEC:], ACT.Exp, scale=-1.0).then_inc(rows_exp, 1)
                act.wait_ge(rows_exp, b + 1)
                act.dma_start(rows_d, rows[0:P:32, :]).then_inc(rows_stored, 16)
                act.dma_start(one(o_sm[bass.ds(b, 1)]), m_deco[:]).then_inc(m_stored, 16)
                act.wait_ge(y_stored, b * 128 + 128)
                w_high(g_blk(b, O_HEAD))
                act.wait_ge(rows_stored, b * 16 + 16)
                with act.Fori(0, 2, 1) as j:
                    for u in range(2):
                        h = j * 2 + u
                        hd = b * 4 + j * 2 + u
                        g = g_head(b, j, u)
                        act.dma_start(x[:, bass.ds(h * 2, 2), :], x_blk[bass.ds(b * KT + h * 2, 2)].rearrange("k p c -> p k c")).then_inc(x_loaded, 16)
                        act.wait_ge(bc_used, hd + 1)
                        act.dma_start(bc, rows_d[bass.ds(h, 1), :].to_broadcast([P, 3 * W + DEC])).then_inc(bc_loaded, 16)
                        w_high(g.at(1))
                        read_out(act, g.at(0))
                        act.activation(qf, qf, ACT.Identity, bias=dyn(C_BIN + u * 7, j * 14)).then_inc(bias_done, 1)
                        act.wait_ge(st_stored, hd * 32 + 32)
                        act.dma_start(ds_dec[:, :, 0:P], one(st_c[bass.ds(hd, 1)]).rearrange("p (s c) -> p s c", s=DEC)).then_inc(c_loaded, 16)
                        act.dma_start(n_dec, one(st_n[bass.ds(hd, 1)])).then_inc(n_loaded, 16)
                        read_out(act, g.at(1))
                        act.activation(kf, kf, ACT.Identity, scale=KSCALE, bias=dyn(C_BK + u, j * 2)).then_inc(bias_done, 1)
                        w_high(g.at(2))
                        read_out(act, g.at(2))
                        act.activation(vf, vf, ACT.Identity, bias=dyn(C_BIN + u * 7 + 2, j * 14)).then_inc(bias_done, 1)
                        act.wait_ge(acol_t, hd + 1)
                        act.activation(a_col.rearrange("p c h -> p (c h)"),
                                       td[:, :].rearrange("p (i r) -> p i r", r=32)[:, :, 0], ACT.Copy).then_inc(acol_done, 1)
                        act.wait_ge(acol_done, hd + 1)
                        act.wait_ge(e_pre, hd + 1)
                        for c in range(CH):
                            act.activation(emat[:, c * P:(c + 1) * P], emat[:, c * P:(c + 1) * P], ACT.Exp,
                                           bias=a_col[:, c, bass.ds(h, 1)]).then_inc(e_done, 1)

                        def ktv_evac(c):
                            act.wait_ge(t_done, hd * CH + (c + 1))
                            if c >= 2:
                                act.wait_ge(n_done, hd * CH + (c - 1))
                            act.activation(ktv[:, c % 2, 0:2 * P], ta[:, c % 2, 0:2 * P], ACT.Copy).then_inc(ktv_done, 1)

                        def nd(c):
                            act.wait_ge(n_done, hd * CH + (c + 1))
                            act.activation(numden[:, :, c * P:(c + 1) * P],
                                           tb[:, 0:2 * P].rearrange("p (a c) -> p a c", a=2), ACT.Copy).then_inc(nd_evac, 1)

                        def lsg(i, *args, **kw):
                            if i:
                                act.wait_ge(a_sig, hd * 3 + i)
                            act.activation(hsq, *args, **kw).then_inc(a_sig, 1)

                        ktv_evac(0)
                        w_high(g.at(3))
                        ktv_evac(1)
                        read_out(act, g.at(3))
                        lsg(0, of, ACT.Abs, bias=dyn(C_BIN + u * 7 + 3, j * 14))
                        nd(0)
                        lsg(1, hsq, ACT.Exp, scale=-1.0)
                        ktv_evac(2)
                        w_high(g.at(4))
                        nd(1)
                        ktv_evac(3)
                        lsg(2, hsq, ACT.Ln, bias=1.0)
                        read_out(act, g.at(4))
                        act.activation(cgb, cgb, ACT.Identity, bias=dyn(C_BIN + u * 7 + 4, j * 14)).then_inc(conv_bias, 1)
                        nd(2)
                        act.wait_ge(td_done, hd + 1)
                        act.activation(dk[0:1, :, 0:2 * P], ta[0:1, 0, :].rearrange("p (s c) -> p s c", s=DEC),
                                       ACT.Copy).then_inc(dk_done, 1)
                        act.wait_ge(sig_pre, hd + 1)
                        act.activation(of, of, ACT.Exp).then_inc(sig_done, 1)
                        w_high(g.at(5))
                        nd(3)
                        act.wait_ge(h_done, hd * 3 + 1)
                        act.activation(hsq[:, 0:2 * P], hraw[:, 0:2 * P], ACT.Square).then_inc(hsq_done, 1)
                        read_out(act, g.at(5))
                        act.activation(cgc, cgc, ACT.Identity, bias=dyn(C_BIN + u * 7 + 5, j * 14)).then_inc(conv_bias, 1)
                        act.wait_ge(dn_done, hd + 1)
                        act.activation(numden[:, :, TOK:W], tb[:, 0:2 * DEC].rearrange("p (a c) -> p a c", a=2),
                                       ACT.Copy).then_inc(dnd_evac, 1)
                        act.wait_ge(h_done, hd * 3 + 3)
                        act.activation(hsq[:, 2 * P:W], hraw[:, 2 * P:W], ACT.Square).then_inc(hsq_done, 1)
                        w_high(g.at(6))
                        read_out(act, g.at(6))
                        act.activation(chc, chc, ACT.Identity, bias=dyn(C_BIN + u * 7 + 6, j * 14)).then_inc(conv_bias, 1)
                        act.wait_ge(hn_done, hd + 1)
                        for bank, (c, wd) in zip((td, tb), GROUPS):
                            a = act.activation(hr[:, c:c + wd], bank[:, 0:wd], ACT.Ln, scale=1.0 / P, bias=col(C_EPS))
                        a.then_inc(a_head, 1)
                        act.wait_ge(a_head, hd + 1)
                        act.activation(hr, hr, ACT.Exp, scale=-0.5).then_inc(hr_done, 1)
                        act.wait_ge(yh_done, hd + 1)
                        act.activation(tile(act_hi, h + 4), hraw, ACT.Copy).then_inc(y_hi, 1)
                        act.wait_ge(yc_done, hd + 1)
                        act.activation(tile(act_hi, h), yc, ACT.Copy).then_inc(y_hi, 1)
                        w_high(g.at(7))
                        act.dma_start(one(o_sc[bass.ds(hd, 1)]).rearrange("p (s c) -> p s c", s=DEC), ds_dec[:, :, 0:P]).then_inc(st_stored, 16)
                        act.dma_start(one(o_sn[bass.ds(hd, 1)]), n_dec).then_inc(st_stored, 16)
                def res_tile(g, e, use, gain):
                    for n, (c, wd) in enumerate(GROUPS):
                        act.wait_ge(res_acc, b * 51 + e * 2 + (use * 17 + n + 1))
                        act.wait_ge(evacuated, g.twice + (n + 5))
                        act.activation(sq_res[:, c:c + wd], cols(x, e, n), ACT.Square).then_inc(res_sq, 1)
                        if gain is not None:
                            act.activation(cols(xn_hi, e, n), cols(x, e, n), ACT.Copy, scale=dyn(gain, e)).then_inc(res_hi, 1)

                def cache(e):
                    act.dma_start(big[:, bass.ds(e * 1024, 1024)], one(kvc_d[bass.ds(b * 8 + e, 1)])).then_inc(cache_loaded, 16)

                act.wait_ge(y_lo, b * 8 + 8)
                act.dma_start(one(o_sconv[bass.ds(b, 1)]), cv_out[:].rearrange("p a b c -> p (a b c)")).then_inc(cv_stored, 16)
                res_tile(g_blk(b, O_OUT), 0, 0, C_GCROSS)
                with act.Fori(0, KT // 2 - 1, 1) as j:
                    for i in range(2):
                        g = g_blk(b, O_OUT, j).at(i + 1)
                        res_tile(g, j * 2 + (i + 1), 0, C_GCROSS)
                        w_high(g)
                        cache(j * 2 + i)
                g = g_blk(b, O_OUT, KT // 2 - 1).at(1)
                res_tile(g, KT - 1, 0, C_GCROSS)
                w_high(g)
                act.wait_ge(st_stored, b * (32 * HEADS) + 32 * (HEADS + 1))
                def exps(h, ts):
                    for t in ts:
                        act.wait_ge(mx_done, b * 8 + (h * 2 + t // 2 + 1))
                        act.activation(prob[:, t, :], ta[:, t // 2, (t % 2) * 256:(t % 2) * 256 + 256], ACT.Exp,
                                       scale=XSCALE, bias=mx[:, t, 1:2], accum_out=mx[:, t, 2:3]).then_inc(exp_done, 1)

                def pt(h, ts):
                    for t in ts:
                        act.wait_ge(pt_done, b * 16 + (h * 4 + t + 1))
                        act.activation(prob_t[:, :, t * P:(t + 1) * P],
                                       (tb, td)[t % 2][:, 0:256].rearrange("p (m c) -> p m c", m=MT),
                                       ACT.Copy).then_inc(pt_evac, 1)

                def out_high(h):
                    for dt, bank in enumerate((tb, td)):
                        act.wait_ge(pv_done, b * 8 + (h * 2 + dt + 1))
                        act.activation(act_hi[:, 2 * h + dt, 0:TOK], bank[:, :], ACT.Copy).then_inc(o_hi, 1)

                w_high(g_blk(b, O_XQ))
                rnorm(r_res, (ta[:, 0, :], ta[:, 1, :]), b * 4 + 2)
                cache(6)
                w_high(g_blk(b, O_XQ).at(1))
                cache(7)
                for h in range(HEADS - 1):
                    exps(h, range(4))
                    w_high(g_blk(b, O_XQ).at(2 * h + 2))
                    pt(h, range(4))
                    w_high(g_blk(b, O_XQ).at(2 * h + 3))
                    out_high(h)
                h = HEADS - 1
                exps(h, (0, 1))
                act.wait_ge(ds_done, b + 1)
                act.activation(s_t, gb[:, 0, 0:16], ACT.Copy).then_inc(ds_evac, 1)
                exps(h, (2, 3))
                pt(h, (0, 1))
                act.wait_ge(dmx_done, b + 1)
                act.activation(pd[0:8, :], gb[0:8, 1, 0:NMEM], ACT.Exp, scale=XSCALE, bias=dmx[0:8, 1:2],
                               accum_out=dmx[0:8, 2:3]).then_inc(dexp_done, 1)
                pt(h, (2, 3))
                act.wait_ge(dpt_done, b + 1)
                act.activation(p_t, gb[:, 2, 0:16], ACT.Copy).then_inc(dpt_evac, 1)
                out_high(h)
                act.wait_ge(dpv_done, b + 1)
                act.activation(act_hi[:, :, TOK:W], gb[:, 3, 0:16].rearrange("p (k i) -> p k i", i=DEC), ACT.Copy).then_inc(do_hi, 1)
                with act.Fori(0, KT // 2, 1) as j:
                    for i in range(2):
                        g = g_blk(b, O_XO, j).at(i)
                        e = j * 2 + i
                        act.dma_start(tile(x_next, e), one(x_blk[bass.ds(b * KT + e + KT, 1)])).then_inc(xnext_loaded, 16)
                        res_tile(g, e, 1, C_GFFN)
                        w_high(g)
                rnorm(r_res, (ta[:, 0, :], ta[:, 1, :]), b * 4 + 3)
                fo = 0
                for gr, size in enumerate(FFG):
                    with act.Fori(0, size, 1) as f:
                        g = g_blk(b, O_FF[gr], f)
                        fi = b * 44 + f * 2 + 2 * fo

                        def e_part(n):
                            c, wd = GROUPS[n]
                            act.wait_ge(evacuated, g.twice + (n + 5))
                            act.activation(et[:, c:c + wd], gt[:, c:c + wd], ACT.Exp, scale=-1.0).then_inc(e_ffn, 1)

                        def h_part(n):
                            c, wd = GROUPS[n]
                            act.wait_ge(h_ffn, fi + (n + 1))
                            act.activation(cols(act_hi, f, n), ht[:, c:c + wd], ACT.Copy).then_inc(hid_hi, 1)

                        e_part(0)
                        w_high(g)
                        e_part(1)
                        h_part(0)
                        w_high(g.at(1))
                        h_part(1)
                    fo += size
                    if gr == len(FFG) - 1:
                        act.wait_ge(xnext_loaded, b * 128 + 144)
                    with act.Fori(0, KT // 2, 1) as j:
                        for i in range(2):
                            g = g_blk(b, O_FF[gr] + 2 * size, j).at(i)
                            if gr == len(FFG) - 1:
                                e = j * 2 + i
                                act.wait_ge(mix_acc, b * 9 + e + 19)
                                act.activation(tile(xn_hi, e), tile(x_next, e), ACT.Copy, scale=dyn(C_GMIX, e)).then_inc(mix_hi, 1)
                                act.activation(sq_mix[:], tile(x_next, e), ACT.Square).then_inc(mix_sq, 1)
                                res_tile(g, e, 2, None)
                            w_high(g)
                rnorm(r_res, (ta[:, 0, :], ta[:, 1, :]), b * 4 + 4)
                for k in range(KT):
                    act.wait_ge(y_ready, b * 8 + (k + 1))
                    act.dma_start(one(y[bass.ds(b * KT + k, 1)]), x[:, k, :]).then_inc(y_stored, 16)
            act.dma_start(o_pconv, carry[:].rearrange("p a b -> p (a b)")).then_inc(out_stored, 16)
            act.dma_start(o_pc, state[:].rearrange("p a b -> p (a b)")).then_inc(out_stored, 16)
            act.dma_start(o_pm, m_st[:]).then_inc(out_stored, 16)
            act.wait_ge(out_stored, 48)
            act.wait_ge(y_stored, 128 * (BLOCKS + 1))
            act.wait_ge(m_stored, 16 * (BLOCKS + 1))
            act.wait_ge(cv_stored, 16 * (BLOCKS + 1))
            act.wait_ge(st_stored, 32 * (BLOCKS * HEADS + 1))
            for i in range(2):
                act.wait_ge(w_loaded[i], 8 * G_ALL + 16)

        @block.vector
        def _(v):
            def col(c):
                return cst[:, c:c + 1]

            def dyn(c, e):
                return cst[:, bass.ds(e + c, 1)]

            v.sem_inc(evacuated, 4)
            for s, n in ((hr_done, 1), (o_lo, 1), (bc_used, 1), (y_stored, 128), (m_stored, 16), (cv_stored, 16),
                         (st_stored, 32)):
                v.sem_inc(s, n)
            v.memset(acc_mix[:], 0.0).then_inc(mix_acc, 1)
            for t, val in ((d0[:], 0.0), (state[:], 0.0), (carry[:], 0.0), (m_st[:], 0.0)):
                v.memset(t, val).then_inc(set_up, 1)
            v.wait_ge(cst_loaded, 32)
            nbias = [(C_BK + h, C_BIN + 7 * h + 1, KSCALE) for h in range(HEADS)]
            for dst, src, f in nbias:
                v.tensor_scalar(col(dst), col(src), f, None, ALU.mult).then_inc(set_up, 1)
            v.wait_ge(set_up, 4 + len(nbias))

            def prep(src, k, gain, hi, lo, hi_sem, hi_count, lo_sem):
                v.wait_ge(hi_sem, hi_count)
                v.scalar_tensor_tensor(out=lo, in0=src, scalar=gain, in1=hi, op0=ALU.mult,
                                       op1=ALU.subtract).then_inc(lo_sem, 1)

            def add_sq(acc, sq, sq_sem, count, acc_sem, acc_count, width=W):
                v.wait_ge(sq_sem, count)
                v.wait_ge(acc_sem, acc_count)
                v.tensor_tensor(acc[:, 0:width], acc[:, 0:width], sq[:, 0:width], ALU.add).then_inc(acc_sem, 1)

            v.wait_ge(memx_loaded, 16)
            for k in range(KT):
                prep(memx[:, k, :], k, col(C_GMEM + k), xn_hi[:, k, 0:NMEM].bitcast(F32), xn_lo[:, k, 0:NMEM],
                     mix_hi, k + 1, mix_lo)
                add_sq(acc_mix, sq_mix, mix_sq, k + 1, mix_acc, k + 1, NMEM)
            v.wait_ge(r_done, 1)
            v.memset(acc_mix[:], 0.0).then_inc(mix_acc, 1)
            for base, dst in ((0, mem_kt), (KT // 2, vfeat)):
                with v.Fori(0, KT // 2, 1) as j:
                    for i in range(2):
                        g = Gemm(j + base, i)
                        v.wait_ge(group_done, g.twice + 2)
                        v.tensor_tensor(tile(dst, j * 2 + i), gb[:, 2 * i, 0:NMEM], r_mix[:, 0:NMEM],
                                        ALU.mult).then_inc(evacuated, 2)
            v.wait_ge(xnext_loaded, 16)
            for k in range(KT):
                prep(x_next[:, k, :], k, col(C_GMIX + k), xn_hi[:, k, :].bitcast(F32), xn_lo[:, k, :],
                     mix_hi, 8 + k + 1, mix_lo)
                add_sq(acc_mix, sq_mix, mix_sq, 8 + k + 1, mix_acc, 9 + k + 1)

            def evac_one(g, n, f):
                v.wait_ge(group_done, g.twice + (n + 1))
                c, wd = GROUPS[n]
                f(slice(c, c + wd), gb[:, 2 * g.slot + n, 0:wd]).then_inc(evacuated, 1)

            def evac(g, f):
                for n in range(2):
                    evac_one(g, n, f)

            def scaled(dst, r):
                return lambda c, ps: v.tensor_tensor(dst[:, c], ps, r[:, c], ALU.mult)

            with v.Fori(0, BLOCKS, 1) as b:
                st = Steps(v, v_gate, b * STEPS["v_gate"], "v_gate", STEPS["v_gate"])
                st(v.memset(ktv[:, :, 2 * P:3 * P], 1.0))
                st(v.memset(dk[0:1, :, 2 * P:3 * P], 1.0))
                g = g_blk(b, O_GATE)
                v.wait_ge(r_done, b * 4 + 2)
                v.memset(acc_mix[:], 0.0).then_inc(mix_acc, 1)
                evac(g, scaled(gi, r_mix))
                evac(g.at(1), scaled(gz, r_mix))
                v.wait_ge(ls_done, b + 1)
                st(v.scalar_tensor_tensor(out=gt1, in0=gz, scalar=0.0, in1=gt1, op0=ALU.min, op1=ALU.subtract))
                st.settle()
                st(v.tensor_tensor_scan(brow, reset, gt1, 0.0, ALU.mult, ALU.add))
                st.settle()
                v.wait_ge(gate_i, b + 1)
                st(v.tensor_tensor(a_row[:], gi, brow, ALU.subtract))
                st(v.tensor_copy(d0[:, P:TOK:P], brow[:, P - 1:TOK - P:P]))
                st.settle()
                v.wait_ge(mdec_loaded, b * 16 + 16)
                v.wait_ge(m_stored, b * 16 + 16)
                v.wait_ge(cv_stored, b * 16 + 16)
                st(v.tensor_tensor_scan(rows[:, 0:TOK], d0[:], a_row[:, 0:TOK], m_st[:, 0:1], ALU.add, ALU.max))
                st(v.tensor_tensor(rows[:, TOK:W], m_dec[:], a_row[:, TOK:W], ALU.max))
                st.settle()
                st(v.tensor_tensor(m_st[:, 1:CH + 1], brow[:, P - 1:TOK:P], rows[:, P - 1:TOK:P], ALU.add))
                st(v.tensor_tensor(rows[:, 2 * W + DEC:], brow, rows[:, 0:W], ALU.add))
                st(v.tensor_tensor(rows[:, W + TOK:2 * W], m_dec[:], rows[:, TOK:W], ALU.subtract))
                st(v.tensor_tensor(rows[:, 2 * W:2 * W + DEC], a_row[:, TOK:W], rows[:, TOK:W], ALU.subtract))
                st(v.tensor_tensor(m_deco[:], brow[:, TOK:W], rows[:, TOK:W], ALU.add))
                st.settle()
                v.tensor_tensor(rows[:, W:W + TOK].rearrange("p (c l) -> p c l", c=CH),
                                m_st[:, 0:CH].rearrange("p (c o) -> p c o", o=1).to_broadcast([P, CH, P]),
                                rows[:, 0:TOK].rearrange("p (c l) -> p c l", c=CH), ALU.subtract).then_inc(rows_pre, 1)
                v.wait_ge(rows_pre, b + 1)
                st(v.tensor_copy(m_st[:, 0:1], m_st[:, CH:CH + 1]))
                st.end()
                with v.Fori(0, 2, 1) as j:
                    for u in range(2):
                        h = j * 2 + u
                        hd = b * 4 + j * 2 + u
                        g = g_head(b, j, u)
                        per = STEPS["v_head"]
                        st = Steps(v, v_head, hd * per, "v_head", per)
                        v.tensor_copy(ws, tile(state, h)).then_inc(state_done, 1)
                        evac(g, scaled(qf, r_mix))
                        evac(g.at(1), scaled(kf, r_mix))
                        v.wait_ge(bc_loaded, hd * 16 + 16)
                        v.tensor_tensor(emat.rearrange("p (c l) -> p c l", c=CH),
                                        maskneg.rearrange("p (o l) -> p o l", o=1).to_broadcast([P, CH, P]),
                                        bc[:, 0:TOK].rearrange("p (c l) -> p c l", c=CH), ALU.subtract).then_inc(e_pre, 1)
                        evac(g.at(2), scaled(vf, r_mix))
                        v.wait_ge(bias_done, hd * 3 + 1)
                        v.tensor_tensor(qg[:, 0:TOK], qf[:, 0:TOK], bc[:, W:W + TOK], ALU.mult).then_inc(qg_done, 1)
                        evac(g.at(3), scaled(of, r_mix))

                        def wv(c):
                            s = c % 2
                            last = emat[:, c * P + P - 1:c * P + P]
                            v.wait_ge(ktv_done, hd * CH + (c + 1))
                            v.wait_ge(e_done, hd * CH + (c + 1))
                            v.tensor_tensor(w_sb[:, s, :], ta[:, s, 2 * P:3 * P], emat[:, c * P:(c + 1) * P],
                                            ALU.mult).then_inc(w_done, 1)
                            v.tensor_scalar(vs_sb[:, s, :], ktv[:, s, P:3 * P], last, None, ALU.mult).then_inc(vs_done, 1)

                        def update(c):
                            decay = bc[:, W + c * P + P - 1:W + c * P + P]
                            v.wait_ge(nd_evac, hd * CH + (c + 1))
                            v.wait_ge(state_done, hd * 5 + (c + 1))
                            v.scalar_tensor_tensor(out=ws, in0=ws, scalar=decay, in1=tb[:, 2 * P:4 * P],
                                                   op0=ALU.mult, op1=ALU.add).then_inc(state_done, 1)

                        def h_cols(c0, c1):
                            num, den = numden[:, 0, c0:c1], numden[:, 1, c0:c1]
                            st(v.scalar_tensor_tensor(out=den, in0=den, scalar=-1.0, in1=den, op0=ALU.mult, op1=ALU.max))
                            st.settle()
                            st(v.tensor_tensor(den, den, bc[:, 2 * W + DEC + c0:2 * W + DEC + c1], ALU.max))
                            st.settle()
                            st(v.reciprocal(den, den))
                            st.settle()
                            v.tensor_tensor(hraw[:, c0:c1], num, den, ALU.mult).then_inc(h_done, 1)

                        wv(0)
                        wv(1)
                        evac_one(g.at(4), 0, scaled(cgb, r_mix))
                        update(0)
                        wv(2)
                        evac_one(g.at(4), 1, scaled(cgb, r_mix))
                        update(1)
                        wv(3)
                        h_cols(0, 2 * P)
                        v.wait_ge(a_sig, hd * 3 + 1)
                        st(v.tensor_scalar(of, of, dyn(C_BIN + u * 7 + 3, j * 14), 0.0, ALU.add, ALU.min))
                        evac_one(g.at(5), 0, scaled(cgc, r_mix))
                        update(2)
                        v.wait_ge(dk_done, hd + 1)
                        for i in range(DEC):
                            a = v.tensor_scalar(dvs[0:1, i, :], dk[0:1, i, P:3 * P], bc[0:1, 2 * W + i:2 * W + i + 1],
                                                None, ALU.mult)
                        a.then_inc(dvs_done, 1)
                        v.wait_ge(a_sig, hd * 3 + 3)
                        st.settle()
                        v.tensor_tensor(of, of, hsq, ALU.subtract).then_inc(sig_pre, 1)
                        evac_one(g.at(5), 1, scaled(cgc, r_mix))
                        update(3)
                        v.wait_ge(c_loaded, hd * 16 + 16)
                        v.wait_ge(n_loaded, hd * 16 + 16)
                        v.wait_ge(state_done, hd * 5 + 5)
                        for i in range(DEC):
                            st(v.tensor_copy(ds_dec[:, i, P:2 * P], n_dec[:, i:i + 1].to_broadcast([P, P])))
                        st(v.tensor_copy(tile(state, h), ws))
                        st.settle()
                        v.wait_ge(dupd_done, hd + 1)
                        for i in range(DEC):
                            st(v.scalar_tensor_tensor(out=ds_dec[:, i, :], in0=ds_dec[:, i, :],
                                                      scalar=bc[:, W + TOK + i:W + TOK + i + 1],
                                                      in1=td[:, i * 256:(i + 1) * 256], op0=ALU.mult, op1=ALU.add))
                        st.settle()
                        v.tensor_copy(n_dec, ds_dec[:, :, P]).then_inc(dstate_done, 1)
                        v.wait_ge(nd_evac, hd * CH + 4)
                        h_cols(2 * P, TOK)
                        evac_one(g.at(6), 0, scaled(chc, r_mix))
                        v.wait_ge(dnd_evac, hd + 1)
                        h_cols(TOK, W)
                        v.wait_ge(h_done, hd * 3 + 3)
                        v.sem_inc(bc_used, 1)
                        evac_one(g.at(6), 1, scaled(chc, r_mix))
                        st(v.tensor_copy(ub[:, 0:2], tile(carry, h)))
                        v.wait_ge(conv_bias, hd * 3 + 3)
                        st(v.tensor_tensor(ub[:, 2:W + 2], cgc, chc, ALU.mult))
                        st.settle()
                        v.wait_ge(cvin_loaded, b * 16 + 16)
                        tap = [dyn(C_CW + 3 * u + i, j * 6) for i in range(3)]
                        cin = cv_in[:, bass.ds(h, 1), :, :].rearrange("p o r i -> p (o r) i")
                        cout = cv_out[:, bass.ds(h, 1), :, :].rearrange("p o r i -> p (o r) i")
                        st(v.tensor_scalar(yc[:, 0:TOK], ub[:, 0:TOK], tap[0], None, ALU.mult))
                        st(v.tensor_scalar(yc[:, TOK:W], cin[:, 0, :], tap[0], None, ALU.mult))
                        st(v.tensor_copy(cout[:, 0, :], cin[:, 1, :]))
                        st(v.tensor_copy(cout[:, 1, :], ub[:, TOK + 2:W + 2]))
                        st(v.tensor_copy(tile(carry, h), ub[:, TOK:TOK + 2]))
                        v.wait_ge(hr_done, hd + 2)
                        st(v.tensor_tensor(hraw, hraw, hr, ALU.mult))
                        st.settle()
                        st(v.scalar_tensor_tensor(out=yc[:, 0:TOK], in0=ub[:, 1:TOK + 1], scalar=tap[1],
                                                  in1=yc[:, 0:TOK], op0=ALU.mult, op1=ALU.add))
                        st(v.scalar_tensor_tensor(out=yc[:, TOK:W], in0=cin[:, 1, :], scalar=tap[1],
                                                  in1=yc[:, TOK:W], op0=ALU.mult, op1=ALU.add))
                        v.wait_ge(sig_done, hd + 1)
                        v.scalar_tensor_tensor(out=hraw, in0=hraw, scalar=dyn(C_GMH + u, j * 2), in1=of,
                                               op0=ALU.mult, op1=ALU.mult).then_inc(yh_done, 1)
                        st.settle()
                        st(v.scalar_tensor_tensor(out=yc, in0=ub[:, 2:W + 2], scalar=tap[2], in1=yc,
                                                  op0=ALU.mult, op1=ALU.add))
                        st.settle()
                        v.tensor_tensor(yc, yc, cgb, ALU.mult).then_inc(yc_done, 1)
                        v.wait_ge(y_hi, hd * 2 + 1)
                        v.tensor_tensor(tile(act_lo, h + 4), hraw, tile(act_hi, h + 4).bitcast(F32),
                                        ALU.subtract).then_inc(y_lo, 1)
                        v.wait_ge(y_hi, hd * 2 + 2)
                        v.tensor_tensor(tile(act_lo, h), yc, tile(act_hi, h).bitcast(F32), ALU.subtract).then_inc(y_lo, 1)
                        st.end()

                def add_x(e):
                    return lambda c, ps: v.tensor_tensor(x_cols(e, c), x_cols(e, c), ps, ALU.add)

                def x_cols(e, c):
                    return x[:, bass.ds(e, 1), c].rearrange("p o c -> p (o c)")

                def res_tile(g, e, use, gain):
                    for n, (c, wd) in enumerate(GROUPS):
                        evac_one(g, n, add_x(e))
                        v.wait_ge(evacuated, g.twice + (n + 5))
                        v.wait_ge(res_sq, b * 48 + e * 2 + (use * 16 + n + 1))
                        v.wait_ge(res_acc, b * 51 + e * 2 + (use * 17 + n + 1))
                        v.tensor_tensor(acc_res[:, c:c + wd], acc_res[:, c:c + wd], sq_res[:, c:c + wd],
                                        ALU.add).then_inc(res_acc, 1)
                        if gain is not None:
                            v.wait_ge(res_hi, b * 32 + e * 2 + (use * 16 + n + 1))
                            v.scalar_tensor_tensor(out=cols(xn_lo, e, n), in0=cols(x, e, n), scalar=dyn(gain, e),
                                                   in1=cols(xn_hi, e, n).bitcast(F32), op0=ALU.mult,
                                                   op1=ALU.subtract).then_inc(res_lo, 1)

                v.wait_ge(x_loaded, b * 64 + 64)
                v.memset(acc_res[:], 0.0).then_inc(res_acc, 1)
                with v.Fori(0, KT // 2, 1) as j:
                    for i in range(2):
                        res_tile(g_blk(b, O_OUT, j).at(i), j * 2 + i, 0, C_GCROSS)
                v.wait_ge(r_done, b * 4 + 3)
                v.memset(acc_res[:], 0.0).then_inc(res_acc, 1)
                per = STEPS["v_att"]
                st = Steps(v, v_att, b * per, "v_att", per)

                def maxima(h):
                    for i in range(2):
                        v.wait_ge(s_done, b * 8 + (h * 2 + i + 1))
                        st(v.tensor_reduce(mx[:, 2 * i:2 * i + 2, 0], ta[:, i, :].rearrange("p (t m) -> p t m", t=2),
                                           AX.X, ALU.max))
                        st.settle()
                        v.tensor_scalar(mx[:, 2 * i:2 * i + 2, 1], mx[:, 2 * i:2 * i + 2, 0], -XSCALE, None,
                                        ALU.mult).then_inc(mx_done, 1)

                def normalise(h, ts):
                    for t in ts:
                        v.wait_ge(exp_done, b * 16 + (h * 4 + t + 1))
                        st(v.reciprocal(mx[:, t, 3:4], mx[:, t, 2:3]))
                        st.settle()
                        v.tensor_scalar(prob[:, t, :], prob[:, t, :], mx[:, t, 3:4], None, ALU.mult).then_inc(p_done, 1)

                def out_low(h):
                    for dt, bank in enumerate((tb, td)):
                        v.wait_ge(o_hi, b * 8 + (h * 2 + dt + 1))
                        v.tensor_tensor(act_lo[:, 2 * h + dt, 0:TOK], bank[:, :],
                                        act_hi[:, 2 * h + dt, 0:TOK].bitcast(F32), ALU.subtract).then_inc(o_lo, 1)

                def xq(m):
                    return g_blk(b, O_XQ).at(m)

                def q_dec(h):
                    read_out(v, xq(2 * h + 1))
                    v.tensor_copy(qd[:, 2 * h:2 * h + 2, :], q_att[:, h % 2, :, TOK:W]).then_inc(qd_done, 1)

                evac(xq(0), scaled(q_att[:, 0, 0, :], r_res))
                evac(xq(1), scaled(q_att[:, 0, 1, :], r_res))
                q_dec(0)
                for h in range(HEADS - 1):
                    s = (h + 1) % 2
                    evac_one(xq(2 * h + 2), 0, scaled(q_att[:, s, 0, :], r_res))
                    maxima(h)
                    normalise(h, range(4))
                    evac_one(xq(2 * h + 2), 1, scaled(q_att[:, s, 0, :], r_res))
                    evac(xq(2 * h + 3), scaled(q_att[:, s, 1, :], r_res))
                    q_dec(h + 1)
                    out_low(h)
                h = HEADS - 1
                maxima(h)
                normalise(h, (0, 1))
                v.wait_ge(dst_done, b + 1)
                st(v.tensor_reduce(dmx[0:8, 0:1], gb[0:8, 1, 0:NMEM], AX.X, ALU.max))
                st.settle()
                v.tensor_scalar(dmx[0:8, 1:2], dmx[0:8, 0:1], -XSCALE, None, ALU.mult).then_inc(dmx_done, 1)
                normalise(h, (2, 3))
                v.wait_ge(dexp_done, b + 1)
                st(v.reciprocal(dmx[0:8, 3:4], dmx[0:8, 2:3]))
                st.settle()
                v.tensor_scalar(pd[0:8, :], pd[0:8, :], dmx[0:8, 3:4], None, ALU.mult).then_inc(dp_done, 1)
                out_low(h)
                st.end()
                v.wait_ge(do_hi, b + 1)
                v.tensor_tensor(act_lo[:, :, TOK:W], gb[:, 3, 0:16].rearrange("p (k i) -> p k i", i=DEC),
                                act_hi[:, :, TOK:W].bitcast(F32), ALU.subtract).then_inc(do_lo, 1)
                with v.Fori(0, KT // 2, 1) as j:
                    for i in range(2):
                        res_tile(g_blk(b, O_XO, j).at(i), j * 2 + i, 1, C_GFFN)
                v.wait_ge(r_done, b * 4 + 4)
                v.memset(acc_res[:], 0.0).then_inc(res_acc, 1)
                fo = 0
                for gr, size in enumerate(FFG):
                    with v.Fori(0, size, 1) as f:
                        g = g_blk(b, O_FF[gr], f)
                        fi = b * 22 + f + fo
                        st = Steps(v, v_ffn, fi * 6, "v_ffn", 6)

                        def part(t, n):
                            c, wd = GROUPS[n]
                            return t[:, c:c + wd]

                        def silu_pre(n):
                            v.wait_ge(e_ffn, fi * 2 + (n + 1))
                            st(v.tensor_scalar(part(et, n), part(et, n), 1.0, None, ALU.add))
                            st.settle()
                            st(v.reciprocal(part(et, n), part(et, n)))

                        def silu(n):
                            st.settle()
                            st(v.tensor_tensor(part(gt, n), part(gt, n), part(et, n), ALU.mult))

                        def hidden(n):
                            v.wait_ge(evacuated, g.at(1).twice + (n + 5))
                            st.settle()
                            v.tensor_tensor(part(ht, n), part(gt, n), part(ut, n), ALU.mult).then_inc(h_ffn, 1)
                            v.wait_ge(hid_hi, fi * 2 + (n + 1))
                            v.tensor_tensor(cols(act_lo, f, n), part(ht, n), cols(act_hi, f, n).bitcast(F32),
                                            ALU.subtract).then_inc(hid_lo, 1)

                        evac_one(g, 0, scaled(gt, r_res))
                        silu_pre(0)
                        evac_one(g, 1, scaled(gt, r_res))
                        silu(0)
                        silu_pre(1)
                        silu(1)
                        evac_one(g.at(1), 0, scaled(ut, r_res))
                        hidden(0)
                        evac_one(g.at(1), 1, scaled(ut, r_res))
                        hidden(1)
                        st.end()
                    fo += size
                    with v.Fori(0, KT // 2, 1) as j:
                        for i in range(2):
                            g = g_blk(b, O_FF[gr] + 2 * size, j).at(i)
                            e = j * 2 + i
                            if gr == len(FFG) - 1:
                                prep(tile(x_next, e), None, dyn(C_GMIX, e), tile(xn_hi, e).bitcast(F32), tile(xn_lo, e),
                                     mix_hi, b * 8 + e + 17, mix_lo)
                                add_sq(acc_mix, sq_mix, mix_sq, b * 8 + e + 17, mix_acc, b * 9 + e + 19)
                                res_tile(g, e, 2, None)
                            else:
                                evac(g, add_x(e))
                v.wait_ge(r_done, b * 4 + 5)
                for k in range(KT):
                    v.scalar_tensor_tensor(out=x[:, k, :], in0=x[:, k, :], scalar=col(C_GFIN + k), in1=r_res[:],
                                           op0=ALU.mult, op1=ALU.mult).then_inc(y_ready, 1)


def kernel(x_prompt, x_sample, mem_prompt, state_conv, state_mlstm_C, state_mlstm_n, state_mlstm_m,
           cache_mem_k, cache_mem_v, g_mix, w_in, b_in, conv_w, g_mh, w_out, g_cross, g_mem,
           w_xq, w_xkv, w_xo, g_ffn, w_gu, w_down, g_final):
    import concourse.bacc as bacc
    from concourse.bass_utils import run_bass_kernel_spmd

    f = np.float32
    A = np.ascontiguousarray

    def feat(a):
        return A(np.asarray(a).T.reshape(KT, P, -1).transpose(1, 0, 2))

    def chunk(w, c0, n=P):
        k = w.shape[0] // P
        out = np.zeros((P, KT, P), f)
        out[:, :k, :n] = w[:, c0:c0 + n].reshape(k, P, n).transpose(1, 0, 2)
        return out.reshape(P, KT * P)

    xp = feat(np.asarray(x_prompt)[0])
    xs = feat(np.asarray(x_sample)[:, 0])
    x_blk = np.zeros((BLOCKS + 1, KT, P, W), f)
    for b in range(BLOCKS):
        x_blk[b, :, :, :TOK] = xp[:, :, b * TOK:(b + 1) * TOK].transpose(1, 0, 2)
        x_blk[b, :, :, TOK:] = xs[:, :, b * DEC:(b + 1) * DEC].transpose(1, 0, 2)
    wi, bi = np.asarray(w_in)[0], np.asarray(b_in)[0]
    C2 = 512
    GO = 7 * C2
    gate_w, gate_b = [], []
    for part in range(2):
        t = np.zeros((D, P), f)
        t[:, ::32] = wi[:, GO + 4 * part:GO + 4 * part + 4]
        gate_w.append(chunk(t, 0))
        v = np.zeros(P, f)
        v[::32] = bi[GO + 4 * part:GO + 4 * part + 4]
        gate_b.append(v)
    order = [(3 + s) * C2 for s in range(4)] + [s * C2 for s in range(3)]
    st = list(gate_w)
    for h in range(HEADS):
        st += [chunk(wi, o + h * P) for o in order]
    for w in (w_out, w_xq, w_xo):
        st += [chunk(np.asarray(w)[0], m * P) for m in range(KT)]
    gu, dn = np.asarray(w_gu)[0], np.asarray(w_down)[0]
    fo = 0
    for size in FFG:
        for i in range(fo, fo + size):
            st += [chunk(gu, i * P), chunk(gu, FF + i * P)]
        st += [chunk(dn[fo * P:(fo + size) * P], m * P) for m in range(KT)]
        fo += size
    w_st = np.stack(st)
    w_kv = np.stack([chunk(np.asarray(w_xkv)[0], m * P) for m in range(2 * KT)])
    cst = np.zeros((P, NCST), f)
    for h in range(HEADS):
        for s, o in enumerate(order):
            cst[:, C_BIN + 7 * h + s] = bi[o + h * P:o + (h + 1) * P]
        cst[:, C_CW + 3 * h:C_CW + 3 * h + 3] = np.asarray(conv_w)[0, :, h * P:(h + 1) * P].T
        cst[:, C_GMH + h] = np.asarray(g_mh)[0, h * P:(h + 1) * P]
    cst[:, C_GI], cst[:, C_GF] = gate_b
    for c, gg in ((C_GMIX, np.asarray(g_mix)[0]), (C_GCROSS, np.asarray(g_cross)[0]), (C_GMEM, np.asarray(g_mem)[0]),
                  (C_GFFN, np.asarray(g_ffn)[0]), (C_GFIN, np.asarray(g_final))):
        cst[:, c:c + KT] = gg.reshape(KT, P).T
    cst[:, C_EPS] = EPS
    idx = np.arange(P)
    mats = np.zeros((P, 3 * P + W), f)
    mats[:, 0:P] = np.eye(P)
    mats[:, P:2 * P] = 1
    mats[:, 2 * P:3 * P] = np.where(idx[:, None] > idx[None, :], MASKED, 0)
    mats[:, 3 * P:] = 1
    mats[:, 3 * P:3 * P + TOK:CHUNK] = 0
    mats[:, 3 * P + TOK:] = 0
    sc = np.asarray(state_conv)[0].reshape(BLOCKS, DEC, 2, HEADS, P)
    st_conv = A(sc.transpose(0, 4, 3, 2, 1)).reshape(BLOCKS, P, HEADS * 2 * DEC)
    c_ = np.asarray(state_mlstm_C)[0].reshape(BLOCKS, DEC, HEADS, P, P)
    st_c = A(c_.transpose(0, 2, 4, 1, 3)).reshape(BLOCKS * HEADS, P, DEC * P)
    n_ = np.asarray(state_mlstm_n)[0].reshape(BLOCKS, DEC, HEADS, P)
    st_n = A(n_.transpose(0, 2, 3, 1)).reshape(BLOCKS * HEADS, P, DEC)
    st_m = np.zeros((BLOCKS, P, DEC), f)
    st_m[:, ::32, :] = np.asarray(state_mlstm_m)[0].reshape(BLOCKS, DEC, HEADS).transpose(0, 2, 1)
    k_ = np.asarray(cache_mem_k)[0].reshape(BLOCKS, DEC, NMEM, HEADS, 2, P)
    kc = k_.transpose(0, 5, 1, 3, 4, 2).reshape(BLOCKS, P, 4, 1024)
    v_ = np.asarray(cache_mem_v)[0].reshape(BLOCKS, DEC, MT, P, D)
    vc = v_.transpose(0, 3, 1, 2, 4).reshape(BLOCKS, P, 4, 1024)
    kvc = A(np.concatenate([kc, vc], 2).transpose(0, 2, 1, 3)).reshape(BLOCKS * 8, P, 1024)

    ins = {"x_blk": x_blk.reshape(-1, P, W), "mem_x": feat(np.asarray(mem_prompt)[0]).reshape(P, -1),
           "w_kv": w_kv, "w_st": w_st, "cst_d": cst, "mats_d": mats, "st_conv": st_conv, "st_c": st_c,
           "st_n": st_n, "st_m": st_m, "kvc_d": kvc}
    outs = {"y": (BLOCKS * KT, P, W), "o_pconv": (P, HEADS * 2), "o_pc": (P, HEADS * 256), "o_pm": (P, CH + 1),
            "o_mk": (P, KT * NMEM), "o_mv": (P, KT * NMEM), "o_sconv": (BLOCKS, P, HEADS * 2 * DEC),
            "o_sc": (BLOCKS * HEADS, P, DEC * P), "o_sn": (BLOCKS * HEADS, P, DEC), "o_sm": (BLOCKS, P, DEC)}
    nc = bacc.Bacc("TRN2", target_bir_lowering=False, num_devices=1)
    aps = {n: nc.dram_tensor(n, a.shape, F32, kind="ExternalInput").ap() for n, a in ins.items()}
    aps.update({n: nc.dram_tensor(n, s, F32, kind="ExternalOutput").ap() for n, s in outs.items()})
    aps["rows_d"] = nc.dram_tensor("rows_d", (HEADS, 3 * W + DEC), F32, kind="Internal").ap()
    trunk(nc, **aps)
    res = run_bass_kernel_spmd(nc, [ins], core_ids=[0]).results[0]

    def tokens(a, n):
        return a.transpose(2, 1, 0).reshape(n, D)

    yb = res["y"].reshape(BLOCKS, KT, P, W).transpose(0, 2, 1, 3)
    y_p = np.concatenate([tokens(yb[b, :, :, :TOK], TOK) for b in range(BLOCKS)])[None]
    y_s = np.concatenate([tokens(yb[b, :, :, TOK:], DEC) for b in range(BLOCKS)])[:, None]
    p_conv = A(res["o_pconv"].reshape(P, HEADS, 2).transpose(2, 1, 0)).reshape(1, 1, 2, C2)
    pc = res["o_pc"].reshape(P, HEADS, 256)
    p_C = A(pc[:, :, 0:P].transpose(1, 2, 0))[None, None]
    p_n = A(pc[:, :, P].T)[None, None]
    p_m = A(res["o_pm"][::32, 0])[None, None]
    mk, mv = (tokens(res[n].reshape(P, KT, NMEM), NMEM).reshape(1, 1, NMEM, HEADS, 256) for n in ("o_mk", "o_mv"))
    s_conv = A(res["o_sconv"].reshape(BLOCKS, P, HEADS, 2, DEC).transpose(0, 4, 3, 2, 1)).reshape(1, NDEC, 2, C2)
    s_C = A(res["o_sc"].reshape(BLOCKS, HEADS, P, DEC, P).transpose(0, 3, 1, 4, 2)).reshape(1, NDEC, HEADS, P, P)
    s_n = A(res["o_sn"].reshape(BLOCKS, HEADS, P, DEC).transpose(0, 3, 1, 2)).reshape(1, NDEC, HEADS, P)
    s_m = A(res["o_sm"][:, ::32, :].transpose(0, 2, 1)).reshape(1, NDEC, HEADS)
    return (A(y_p), A(y_s), p_conv, p_C, p_n, p_m, A(mk), A(mv), s_conv, s_C, s_n, s_m)
```

```python
from contextlib import ExitStack

import numpy as np
import concourse.bass as bass
from concourse import mybir

F32 = mybir.dt.float32
F32R = mybir.dt.float32r
ALU = mybir.AluOpType
ACT = mybir.ActivationFunctionType
AX = mybir.AxisListType

P = 128
D = 1024
KT = D // P
SEQ = 2048
NDEC = 8
BLOCKS = 4
TOK = SEQ // BLOCKS
DEC = NDEC // BLOCKS
W = TOK + DEC
GROUPS = [(0, 258), (258, W - 258)]
HEADS = 4
NMEM = 256
MT = NMEM // P
CHUNK = 128
CH = TOK // CHUNK
FF = 2816
FFG = [8, 7, 7]
EPS = 1e-6
KSCALE = P ** -0.5
XSCALE = 256 ** -0.5
MASKED = -1e30

G_KV = 16
O_GATE = 0
O_HEAD = 2
PER_HEAD = 7
O_OUT = O_HEAD + HEADS * PER_HEAD
O_XQ = O_OUT + KT
O_XO = O_XQ + KT
O_FF = []
_o = O_XO + KT
for _n in FFG:
    O_FF.append(_o)
    _o += 2 * _n + KT
G_BLK = _o
G_ALL = G_KV + BLOCKS * G_BLK

C_BIN = 0
C_BK = 32
C_GI, C_GF = 36, 37
C_CW = 38
C_GMH = 50
C_GMIX, C_GCROSS, C_GMEM, C_GFFN, C_GFIN = 54, 62, 70, 78, 86
C_EPS = 94
NCST = 96

STEPS = {"v_gate": 15, "v_head": 31, "v_att": 28}


class Steps:

    def __init__(self, eng, sem, base, name, per):
        self.eng, self.sem, self.base, self.n, self.name, self.per = eng, sem, base, 0, name, per

    def __call__(self, ins):
        ins.then_inc(self.sem, 1)
        self.n += 1

    def settle(self):
        self.eng.wait_ge(self.sem, self.base + self.n)

    def end(self):
        if self.per != self.n:
            raise ValueError(f"{self.name}: {self.n} steps, declared {self.per}")


class Gemm:

    def __init__(self, half, k=0):
        self.half, self.k = half + k // 2, k % 2

    def at(self, k):
        return Gemm(self.half, self.k + k)

    @property
    def slot(self):
        return self.k

    @property
    def twice(self):
        return self.half * 4 + 2 * self.k


def trunk(nc, x_blk, mem_x, w_kv, w_st, cst_d, mats_d, st_conv, st_c, st_n, st_m, kvc_d,
          y, o_pconv, o_pc, o_pm, o_mk, o_mv, o_sconv, o_sc, o_sn, o_sm, rows_d):
    with ExitStack() as ctx:
        def sb(name, shape, dt=F32):
            return ctx.enter_context(nc.sbuf_tensor(name, shape, dt))

        def sem(name):
            return ctx.enter_context(nc.semaphore(name))

        def one(ap):
            return ap.rearrange("o p c -> (o p) c")

        x = sb("x", [P, KT, W])
        xn_hi = sb("xn_hi", [P, KT, W], F32R)
        xn_lo = sb("xn_lo", [P, KT, W], F32R)
        act_hi = sb("act_hi", [P, KT, W], F32R)
        act_lo = sb("act_lo", [P, KT, W], F32R)
        w_raw = sb("w_raw", [P, 2, D])
        w_hi = sb("w_hi", [P, 2, D], F32R)
        w_lo = sb("w_lo", [P, 2, D], F32R)
        mem_k_hi = sb("mem_k_hi", [P, KT, NMEM], F32R)
        mem_k_lo = sb("mem_k_lo", [P, KT, NMEM], F32R)
        mem_v = sb("mem_v", [P, MT, D])
        big = sb("big", [P, 8232])
        work = sb("work", [P, 6664])
        state = sb("state", [P, HEADS, 256])
        r_mix = sb("r_mix", [P, W])
        r_res = sb("r_res", [P, W])
        acc_mix = sb("acc_mix", [P, W])
        acc_res = sb("acc_res", [P, W])
        sq_res = sb("sq_res", [P, W])
        cst = sb("cst", [P, NCST])
        mats = sb("mats", [P, 3 * P + W])
        ident, ones, maskneg = (mats[:, i * P:(i + 1) * P] for i in range(3))
        reset = mats[:, 3 * P:3 * P + W]
        a_row = sb("a_row", [P, W])
        lnt = a_row
        carry = sb("carry", [P, HEADS, 2])
        m_st = sb("m_st", [P, CH + 1])
        m_dec = sb("m_dec", [P, DEC])
        m_deco = sb("m_deco", [P, DEC])
        cv_in = sb("cv_in", [P, HEADS, 2, DEC])
        cv_out = sb("cv_out", [P, HEADS, 2, DEC])

        cursor = {"big": 0, "work": 0}

        def cut(which, n, reset_to=None):
            if reset_to is not None:
                cursor[which] = reset_to
            a = cursor[which]
            cursor[which] = a + n
            t = big if which == "big" else work
            return t[:, a:a + n]

        qf, kf, vf, of = (cut("big", W) for _ in range(4))
        qg = cut("big", W)
        d0 = qg[:, 0:TOK]
        emat = cut("big", TOK)
        numden = cut("big", 2 * W).rearrange("p (a c) -> p a c", a=2)
        cgb, cgc, chc = (cut("big", W) for _ in range(3))
        ub = cut("big", W + 2)
        yc = cut("big", W)
        bc = cut("big", 3 * W + DEC)
        rows = bc
        gi, gz, gt1, brow = cgb, cgc, chc, yc
        V1 = P + 1
        ktv = cut("work", 2 * (P + V1)).rearrange("p (s c) -> p s c", s=2)
        w_sb = cut("work", 2 * P).rearrange("p (s c) -> p s c", s=2)
        vs_sb = cut("work", 2 * V1).rearrange("p (s c) -> p s c", s=2)
        ws = cut("work", 256)
        ds_dec = cut("work", DEC * 256).rearrange("p (s c) -> p s c", s=DEC)
        dk = cut("work", DEC * (P + V1)).rearrange("p (s c) -> p s c", s=DEC)
        dvs = cut("work", DEC * V1).rearrange("p (s c) -> p s c", s=DEC)
        a_col = cut("work", CH * HEADS).rearrange("p (c h) -> p c h", c=CH)
        n_dec = cut("work", DEC)
        hraw = cut("work", W)
        hsq = cut("work", W)
        hr = cut("work", W)
        kc = big[:, 0:4096].rearrange("p (i m) -> p i m", m=NMEM)
        vc = big[:, 4096:8192].rearrange("p (i d) -> p i d", d=D)
        q_att = cut("work", 2 * 2 * W, 0).rearrange("p (s t c) -> p s t c", s=2, t=2)
        prob = cut("work", 4 * NMEM).rearrange("p (s m) -> p s m", s=4)
        prob_t = cut("work", MT * TOK).rearrange("p (t c) -> p t c", t=MT)
        mx = cut("work", 16).rearrange("p (s c) -> p s c", s=4)
        qz = cut("work", 16 * 8)
        pd = cut("work", NMEM)
        pz = cut("work", 32).rearrange("p (t i c) -> p t i c", t=MT, i=DEC)
        o_sb = work[:, 4 * W:4 * W + D]
        dmx = cut("work", 4)
        x_next = big[:, 0:KT * W].rearrange("p (k c) -> p k c", k=KT)
        gt = cut("work", W, 0)
        ut = cut("work", W)
        et = cut("work", W)
        ht = cut("work", W)
        sq_mix = cut("work", W)
        memx = x[:, :, 0:NMEM]
        mem_k = x[:, :, NMEM:2 * NMEM]
        vfeat = work[:, 6664 - KT * NMEM:].rearrange("p (k m) -> p k m", k=KT)

        gb = ctx.enter_context(nc.psum_tensor("gb", [P, 4, 512], F32))
        ta = ctx.enter_context(nc.psum_tensor("ta", [P, 2, 512], F32))
        tb = ctx.enter_context(nc.psum_tensor("tb", [P, 512], F32))
        td = ctx.enter_context(nc.psum_tensor("td", [P, 512], F32))

        def sems(names):
            return [sem(n) for n in names.split()]

        cst_loaded, mats_loaded, memx_loaded, xnext_loaded, x_loaded, set_up = sems(
            "cst_loaded mats_loaded memx_loaded xnext_loaded x_loaded set_up")
        w_loaded = sems("w_loaded_even w_loaded_odd")
        w_hi_done, w_lo_done, group_done, evacuated = sems("w_hi_done w_lo_done group_done evacuated")
        mix_hi, mix_sq, mix_lo, mix_acc = sems("mix_hi mix_sq mix_lo mix_acc")
        res_hi, res_sq, res_lo, res_acc = sems("res_hi res_sq res_lo res_acc")
        ssq_done, ln_done, r_done = sems("ssq_done ln_done r_done")
        v_gate, v_head, v_att, v_ffn = sems("v_gate v_head v_att v_ffn")
        a_gate, a_head = sems("a_gate a_head")
        gate_i, ls_done, rows_pre, rows_exp, rows_stored = sems("gate_i ls_done rows_pre rows_exp rows_stored")
        bc_loaded, bc_used, c_loaded, n_loaded, st_stored = sems("bc_loaded bc_used c_loaded n_loaded st_stored")
        bias_done, acol_t, acol_done, e_pre, e_done = sems("bias_done acol_t acol_done e_pre e_done")
        t_done, ktv_done, w_done, vs_done, qg_done = sems("t_done ktv_done w_done vs_done qg_done")
        n_done, nd_evac, state_done = sems("n_done nd_evac state_done")
        td_done, dk_done, dvs_done, dupd_done, dstate_done, dn_done, dnd_evac = sems(
            "td_done dk_done dvs_done dupd_done dstate_done dn_done dnd_evac")
        h_done, hsq_done, hn_done, hr_done, a_sig, sig_pre, sig_done = sems("h_done hsq_done hn_done hr_done a_sig sig_pre sig_done")
        conv_bias, yc_done, yh_done, y_hi, y_lo = sems("conv_bias yc_done yh_done y_hi y_lo")
        cache_loaded, s_done, mx_done, exp_done, p_done, pt_done, pt_evac = sems(
            "cache_loaded s_done mx_done exp_done p_done pt_done pt_evac")
        pv_done, o_hi, o_lo, qd_done, do_hi, do_lo = sems("pv_done o_hi o_lo qd_done do_hi do_lo")
        ds_done, dmx_done, dexp_done, dp_done, dpt_done, dpt_evac, dpv_done, do_evac, dot_done = sems(
            "ds_done dmx_done dexp_done dp_done dpt_done dpt_evac dpv_done do_evac dot_done")
        dp_seen, mem_hi, q_hi_done, q_lo_done = sems("dp_seen mem_hi q_hi_done q_lo_done")
        e_ffn, h_ffn, hid_hi, hid_lo = sems("e_ffn h_ffn hid_hi hid_lo")
        y_ready, y_stored, out_stored, vt_done, vt_evac, kv_stored = sems(
            "y_ready y_stored out_stored vt_done vt_evac kv_stored")
        m_stored, mdec_loaded, cvin_loaded, cv_stored = sems("m_stored mdec_loaded cvin_loaded cv_stored")

        def g_head(b, j, u):
            return Gemm(b * (G_BLK // 2) + j * PER_HEAD + (G_KV + O_HEAD) // 2, u * PER_HEAD)

        def g_blk(b, off, j=0):
            return Gemm(b * (G_BLK // 2) + j + (G_KV + off) // 2)

        def read_out(eng, g):
            eng.wait_ge(evacuated, g.twice + 6)

        def tile(t, e, n=1):
            return t[:, bass.ds(e, 1), :].rearrange("p o c -> p (o c)")

        def cols(t, e, n):
            c, wd = GROUPS[n]
            return t[:, bass.ds(e, 1), c:c + wd].rearrange("p o c -> p (o c)")

        dec_cols = [((slice(None), slice(dt, KT, 2), TOK + i), slice(8 * dt + 4 * i, 8 * dt + 4 * i + 52, 17))
                    for dt in range(2) for i in range(DEC)]

        block = ctx.enter_context(nc.Block())

        @block.sync
        def _(sp):
            sp.dma_start(cst[:], cst_d).then_inc(cst_loaded, 16)
            sp.dma_start(memx, mem_x.rearrange("p (k c) -> p k c", k=KT)).then_inc(memx_loaded, 16)
            for i in range(2):
                sp.dma_start(w_raw[:, i, :], w_kv[i]).then_inc(w_loaded[i], 16)
            sp.dma_start(mats[:], mats_d).then_inc(mats_loaded, 16)
            with sp.Fori(1, G_KV // 2, 1) as j:
                for i in range(2):
                    sp.wait_ge(w_lo_done, j * 2 + i - 1)
                    sp.dma_start(w_raw[:, i, :], one(w_kv[bass.ds(j * 2 + i, 1)])).then_inc(w_loaded[i], 16)
            with sp.Fori(0, BLOCKS, 1) as b:
                with sp.Fori(0, G_BLK // 2, 1) as j:
                    for i in range(2):
                        sp.wait_ge(w_lo_done, b * G_BLK + j * 2 + (G_KV + i - 1))
                        sp.dma_start(w_raw[:, i, :], one(w_st[bass.ds(j * 2 + i, 1)])).then_inc(w_loaded[i], 16)
            for i in range(2):
                sp.wait_ge(w_lo_done, G_ALL + i - 1)
                sp.dma_start(w_raw[:, i, :], w_kv[i]).then_inc(w_loaded[i], 16)

        @block.gpsimd
        def _(pool):
            with pool.Fori(G_KV // 2 + 1, G_ALL // 2 + 1, 1) as j:
                for i in range(2):
                    pool.wait_ge(w_hi_done, j * 2 + i + 1)
                    pool.tensor_tensor(w_lo[:, i, :], w_raw[:, i, :], w_hi[:, i, :].bitcast(F32),
                                       ALU.subtract).then_inc(w_lo_done, 1)

        @block.tensor
        def _(pe):
            def group(g, n, col, wd, hi, lo, ks, kwait=None, inc=1, first=True, last=True):
                s = g.slot
                if first:
                    pe.wait_ge(evacuated, g.twice + n + inc)
                for k in ks:
                    if kwait is not None:
                        kwait(k, n)
                    for i, (a, r) in enumerate([(w_hi, hi), (w_hi, lo), (w_lo, hi)]):
                        mm = pe.matmul(gb[:, 2 * s + n, 0:wd], a[:, s, k * P:(k + 1) * P],
                                       r[:, k, col:col + wd], start=(first and k == ks[0] and i == 0),
                                       stop=(last and k == ks[-1] and i == 2))
                if last:
                    mm.then_inc(group_done, inc)

            def split_ready(g):
                pe.wait_ge(w_lo_done, g.half * 2 + g.k + 1)

            def gemm(g, hi, lo, kts=KT, kwait=None, after=(None, None)):
                split_ready(g)
                for n, (col, wd) in enumerate(GROUPS):
                    group(g, n, col, wd, hi, lo, range(kts), kwait)
                    if after[n]:
                        after[n]()

            def sumsq(acc, banks, width=W):
                parts = GROUPS if width == W else [(0, width)]
                for bank, (col, wd) in zip(banks, parts):
                    mm = pe.matmul(bank[:, 0:wd], ones, acc[:, col:col + wd], start=True, stop=True)
                mm.then_inc(ssq_done, 1)

            pe.wait_ge(mats_loaded, 16)

            def kv(g):
                split_ready(g)
                group(g, 0, 0, NMEM, act_hi, act_lo, range(KT), kwait=lambda k, n: pe.wait_ge(mix_lo, k + 1), inc=2)

            kv(Gemm(0))
            pe.wait_ge(mix_acc, 9)
            sumsq(acc_mix, (td, tb), NMEM)
            kv(Gemm(0, 1))
            with pe.Fori(1, G_KV // 2, 1) as j:
                for i in range(2):
                    kv(Gemm(j, i))
            pe.wait_ge(evacuated, 2 * G_KV + 4)
            for q in range(4):
                if q >= 2:
                    pe.wait_ge(vt_evac, q - 1)
                for mt in range(MT):
                    for i in range(2):
                        t = pe.transpose(ta[:, q % 2, mt * 256 + i * P:mt * 256 + (i + 1) * P],
                                         vfeat[:, 2 * q + i, mt * P:(mt + 1) * P], ident)
                t.then_inc(vt_done, 1)
            pe.wait_ge(vt_evac, 4)

            pe.wait_ge(mix_acc, 18)
            sumsq(acc_mix, (td, tb))
            with pe.Fori(0, BLOCKS, 1) as b:
                for i in range(2):
                    gemm(g_blk(b, O_GATE).at(i), xn_hi, xn_lo,
                         kwait=lambda k, n: n or pe.wait_ge(mix_lo, b * 8 + (8 + k + 1)))
                with pe.Fori(0, 2, 1) as j:
                    for u in range(2):
                        hd = b * 4 + j * 2 + u

                        def acols():
                            pe.wait_ge(rows_pre, b + 1)
                            pe.wait_ge(hr_done, hd + 1)
                            for c in range(CH):
                                mm = pe.matmul(td[:, c * HEADS:(c + 1) * HEADS], a_row[:, c * P:(c + 1) * P],
                                               ident[:, 0:P:32], start=True, stop=True)
                            mm.then_inc(acol_t, 1)

                        def t_part(c):
                            bank = ta[:, c % 2, :]
                            if c == 0:
                                pe.wait_ge(bias_done, hd * 3 + 3)
                            if c >= 2:
                                pe.wait_ge(ktv_done, hd * CH + (c - 1))
                                pe.wait_ge(w_done, hd * CH + (c - 1))
                            sl = slice(c * P, (c + 1) * P)
                            pe.transpose(bank[:, 0:P], kf[:, sl], ident)
                            pe.transpose(bank[:, P:2 * P], vf[:, sl], ident)
                            pe.matmul(bank[:, 2 * P:3 * P], kf[:, sl], qf[:, sl],
                                      start=True, stop=True).then_inc(t_done, 1)

                        def n_part(c):
                            sl = slice(c * P, (c + 1) * P)
                            s = c % 2
                            pe.wait_ge(ktv_done, hd * CH + (c + 1))
                            pe.wait_ge(w_done, hd * CH + (c + 1))
                            pe.wait_ge(vs_done, hd * CH + (c + 1))
                            if c == 0:
                                pe.wait_ge(qg_done, hd + 1)
                            else:
                                pe.wait_ge(nd_evac, hd * CH + c)
                            pe.wait_ge(state_done, hd * 5 + (c + 1))
                            pe.matmul(tb[:, 0:P], ws[:, 0:P], qg[:, sl], start=True, stop=False)
                            pe.matmul(tb[:, 0:P], ktv[:, s, P:2 * P], w_sb[:, s, :], start=False, stop=True)
                            pe.matmul(tb[:, P:2 * P], ws[:, P:2 * P], qg[:, sl], start=True, stop=False)
                            pe.matmul(tb[:, P:2 * P], ones, w_sb[:, s, :], start=False, stop=True)
                            pe.matmul(tb[:, 2 * P:2 * P + V1], ktv[:, s, 0:P], vs_sb[:, s, :],
                                      start=True, stop=True).then_inc(n_done, 1)

                        def tdec():
                            pe.wait_ge(ktv_done, hd * CH + 3)
                            pe.wait_ge(w_done, hd * CH + 3)
                            for i in range(DEC):
                                pe.transpose(ta[0:1, 0, i * 256:i * 256 + P], kf[:, TOK + i:TOK + i + 1], ident)
                                t = pe.transpose(ta[0:1, 0, i * 256 + P:i * 256 + 2 * P],
                                                 vf[:, TOK + i:TOK + i + 1], ident)
                            t.then_inc(td_done, 1)

                        def dupd():
                            pe.wait_ge(dvs_done, hd + 1)
                            pe.wait_ge(acol_done, hd + 1)
                            for i in range(DEC):
                                mm = pe.matmul(td[:, i * 256:i * 256 + V1], dk[0:1, i, 0:P], dvs[0:1, i, :],
                                               start=True, stop=True)
                            mm.then_inc(dupd_done, 1)

                        def dnum():
                            pe.wait_ge(dstate_done, hd + 1)
                            pe.wait_ge(state_done, hd * 5 + 5)
                            for i in range(DEC):
                                q1 = qf[:, TOK + i:TOK + i + 1]
                                pe.matmul(tb[:, i:i + 1], ds_dec[:, i, 0:P], q1, start=True, stop=True)
                                mm = pe.matmul(tb[:, DEC + i:DEC + i + 1], ds_dec[:, i, P:2 * P], q1,
                                               start=True, stop=True)
                            mm.then_inc(dn_done, 1)

                        def hnorm():
                            pe.wait_ge(hsq_done, hd * 2 + 2)
                            pe.wait_ge(dnd_evac, hd + 1)
                            pe.matmul(td[:, 0:GROUPS[0][1]], ones, hsq[:, 0:GROUPS[0][1]], start=True, stop=True)
                            pe.matmul(tb[:, 0:GROUPS[1][1]], ones, hsq[:, GROUPS[1][0]:W],
                                      start=True, stop=True).then_inc(hn_done, 1)

                        g = g_head(b, j, u)
                        for i in range(3):
                            gemm(g.at(i), xn_hi, xn_lo)
                        gemm(g.at(3), xn_hi, xn_lo,
                             after=(lambda: (acols(), t_part(0)), lambda: t_part(1)))
                        gemm(g.at(4), xn_hi, xn_lo,
                             after=(lambda: (n_part(0), t_part(2)), lambda: (n_part(1), t_part(3))))
                        gemm(g.at(5), xn_hi, xn_lo,
                             after=(lambda: (n_part(2), tdec()), lambda: (n_part(3), dupd())))
                        gemm(g.at(6), xn_hi, xn_lo, after=(dnum, hnorm))

                def y_wait(k, n):
                    pe.wait_ge(y_lo, b * 8 + (2 * (k % 4) + 2 - k // 4))

                p0, p1 = g_blk(b, O_OUT), g_blk(b, O_OUT).at(1)
                early, late = (0, 1, 2, 4, 5, 6), (7, 3)
                first_three = [(p0, 0), (p0, 1), (p1, 0)]
                for g, n in first_three:
                    split_ready(g)
                    group(g, n, *GROUPS[n], act_hi, act_lo, early, y_wait if (g, n) == (p0, 0) else None, last=False)
                for g, n in first_three:
                    group(g, n, *GROUPS[n], act_hi, act_lo, late, y_wait if (g, n) == (p0, 0) else None, first=False)
                group(p1, 1, *GROUPS[1], act_hi, act_lo, range(KT))
                with pe.Fori(1, KT // 2, 1) as j:
                    for i in range(2):
                        gemm(g_blk(b, O_OUT, j).at(i), act_hi, act_lo)
                def sum_res(use):
                    for n in range(2):
                        pe.wait_ge(res_acc, b * 51 + (use * 17 + 16 + n))
                        c, wd = GROUPS[n]
                        mm = pe.matmul(ta[:, n, 0:wd], ones, acc_res[:, c:c + wd], start=True, stop=True)
                    mm.then_inc(ssq_done, 1)

                def res_wait(use):
                    return lambda k, n: pe.wait_ge(res_lo, b * 32 + (use * 16 + 2 * k + n + 1))

                def xq(m, after=(None, None)):
                    gemm(g_blk(b, O_XQ).at(m), xn_hi, xn_lo, kwait=None if m else res_wait(0), after=after)

                def scores(h):
                    pe.wait_ge(q_lo_done, b * 8 + (2 * h + 2))
                    for t in range(CH):
                        for dt in range(2):
                            for i, (q, key) in enumerate([(act_hi, mem_k_hi), (act_hi, mem_k_lo), (act_lo, mem_k_hi)]):
                                mm = pe.matmul(ta[:, t // 2, (t % 2) * 256:(t % 2) * 256 + 256],
                                               q[:, 2 * h + dt, t * P:(t + 1) * P], key[:, 2 * h + dt, :],
                                               start=(dt == 0 and i == 0), stop=(dt == 1 and i == 2))
                        if t % 2:
                            mm.then_inc(s_done, 1)

                def ptrans(h, ts):
                    for t in ts:
                        pe.wait_ge(p_done, b * 16 + (h * 4 + t + 1))
                        if t >= 2:
                            pe.wait_ge(pt_evac, b * 16 + (h * 4 + t - 1))
                        else:
                            pe.wait_ge(o_lo, b * 8 + (h * 2 + 1))
                        for mt in range(MT):
                            m = pe.transpose((tb, td)[t % 2][:, mt * P:(mt + 1) * P],
                                             prob[:, t, mt * P:(mt + 1) * P], ident)
                        m.then_inc(pt_done, 1)

                def pv(h):
                    pe.wait_ge(pt_evac, b * 16 + (h * 4 + 4))
                    for dt, bank in enumerate((tb, td)):
                        for mt in range(MT):
                            mm = pe.matmul(bank[:, :], mem_v[:, mt, h * 256 + dt * P:h * 256 + (dt + 1) * P],
                                           prob_t[:, mt, :], start=(mt == 0), stop=(mt == MT - 1))
                        mm.then_inc(pv_done, 1)

                def dec_scores():
                    pe.wait_ge(cache_loaded, b * 128 + 128)
                    pe.wait_ge(qd_done, b * 4 + 4)
                    for c in range(16):
                        mm = pe.matmul(gb[0:8, 0, 0:NMEM], qz[:, c * 8:(c + 1) * 8], kc[:, c, :],
                                       start=(c == 0), stop=(c == 15))
                    mm.then_inc(ds_done, 1)

                def dec_ptrans():
                    pe.wait_ge(dp_done, b + 1)
                    pe.sem_inc(dp_seen, 1)
                    for mt in range(MT):
                        m = pe.transpose(gb[:, 2, mt * 8:mt * 8 + 8], pd[0:8, mt * P:(mt + 1) * P], ident[0:8, 0:8])
                    m.then_inc(dpt_done, 1)

                def dec_pv():
                    pe.wait_ge(dpt_evac, b + 1)
                    for half in range(2):
                        for c in range(DEC * MT):
                            i, mt = c // MT, c % MT
                            mm = pe.matmul(ta[0:8, half, :], pz[:, mt, i, :], vc[:, c, half * 512:(half + 1) * 512],
                                           start=(c == 0), stop=(c == DEC * MT - 1))
                        mm.then_inc(dpv_done, 1)

                def dec_out(k, n):
                    if (k, n) == (KT - 3, 0):
                        pe.wait_ge(do_evac, b * 2 + 2)
                        pe.sem_inc(dp_seen, 1)
                        for kt in range(KT):
                            m = pe.transpose(gb[:, 3, kt * 8:kt * 8 + 8], o_sb[0:8, kt * P:(kt + 1) * P], ident[0:8, 0:8])
                        m.then_inc(dot_done, 1)
                    if (k, n) == (KT - 2, 0):
                        pe.wait_ge(o_lo, b * 8 + 9)
                    if (k, n) == (0, 1):
                        pe.wait_ge(do_lo, b + 1)

                xq(0, after=(lambda: sum_res(0), None))
                xq(1)
                for h in range(HEADS - 1):
                    xq(2 * h + 2, after=(lambda: scores(h), lambda: ptrans(h, (0, 1))))
                    xq(2 * h + 3, after=(lambda: ptrans(h, (2, 3)), lambda: pv(h)))
                h = HEADS - 1
                scores(h)
                dec_scores()
                ptrans(h, range(4))
                dec_ptrans()
                pv(h)
                dec_pv()
                for i in range(2):
                    gemm(g_blk(b, O_XO).at(i), act_hi, act_lo, kwait=None if i else dec_out)
                with pe.Fori(1, KT // 2, 1) as j:
                    for i in range(2):
                        gemm(g_blk(b, O_XO, j).at(i), act_hi, act_lo)
                def gu(gr, f, after=(None, None)):
                    g = g_blk(b, O_FF[gr], f)
                    gemm(g.at(0), xn_hi, xn_lo, kwait=None if gr else res_wait(1), after=after)
                    gemm(g.at(1), xn_hi, xn_lo)

                gu(0, 0, after=(lambda: sum_res(1), None))
                fo = 0
                for gr, size in enumerate(FFG):
                    with pe.Fori(0 if gr else 1, size, 1) as f:
                        gu(gr, f)
                    with pe.Fori(0, KT // 2, 1) as j:
                        for i in range(2):
                            gemm(g_blk(b, O_FF[gr] + 2 * size, j).at(i), act_hi, act_lo, kts=size,
                                 kwait=(lambda k, n: pe.wait_ge(hid_lo, b * 44 + (2 * (fo + k) + n + 1)))
                                 if i == 0 else None)
                    fo += size
                pe.wait_ge(mix_acc, b * 9 + 27)
                sumsq(acc_mix, (td, tb))
                sum_res(2)

        @block.scalar
        def _(act):
            act.preload_act_table_set("natural_log_exp_and_others")

            def w_high(g):
                s = g.slot
                act.wait_ge(w_loaded[s], g.half * 16 + 32)
                act.wait_ge(group_done, g.twice + 2)
                act.activation(w_hi[:, s, :], w_raw[:, s, :], ACT.Copy).then_inc(w_hi_done, 1)

            def col(c):
                return cst[:, c:c + 1]

            def dyn(c, e):
                return cst[:, bass.ds(e + c, 1)]

            def rnorm(r, banks, index, width=W):
                act.wait_ge(ssq_done, index + 1)
                parts = GROUPS if width == W else [(0, width)]
                for bank, (c, wd) in zip(banks, parts):
                    a = act.activation(lnt[:, c:c + wd], bank[:, 0:wd], ACT.Ln, scale=1.0 / D, bias=col(C_EPS))
                a.then_inc(ln_done, 1)
                act.wait_ge(ln_done, index + 1)
                act.activation(r[:, 0:width], lnt[:, 0:width], ACT.Exp, scale=-0.5).then_inc(r_done, 1)

            act.wait_ge(cst_loaded, 16)
            act.wait_ge(memx_loaded, 16)
            act.dma_start(x_next, x_blk[0:KT].rearrange("k p c -> p k c")).then_inc(xnext_loaded, 16)
            for k in range(KT):
                act.activation(act_hi[:, k, 0:NMEM], memx[:, k, :], ACT.Copy, scale=col(C_GMEM + k)).then_inc(mix_hi, 1)
                act.wait_ge(mix_acc, k + 1)
                act.activation(sq_mix[:, 0:NMEM], memx[:, k, :], ACT.Square).then_inc(mix_sq, 1)
                if k < 2:
                    act.wait_ge(w_loaded[k], 16)
                    act.activation(w_hi[:, k, :], w_raw[:, k, :], ACT.Copy).then_inc(w_hi_done, 1)
            rnorm(r_mix, (td, tb), 0, NMEM)
            act.wait_ge(xnext_loaded, 16)
            with act.Fori(0, G_KV // 2, 1) as j:
                for i in range(2):
                    w_high(Gemm(j, i))
                act.wait_ge(mix_acc, j + 10)
                act.activation(tile(xn_hi, j), tile(x_next, j), ACT.Copy, scale=dyn(C_GMIX, j)).then_inc(mix_hi, 1)
                act.activation(sq_mix[:], tile(x_next, j), ACT.Square).then_inc(mix_sq, 1)
            act.wait_ge(evacuated, 2 * G_KV + 4)
            act.dma_start(o_mk.rearrange("p (k m) -> p k m", k=KT), mem_k).then_inc(kv_stored, 16)
            act.dma_start(o_mv, vfeat.rearrange("p k m -> p (k m)")).then_inc(kv_stored, 16)
            for q in range(4):
                act.wait_ge(vt_done, q + 1)
                act.activation(mem_v[:, :, q * 256:(q + 1) * 256],
                               ta[:, q % 2, :].rearrange("p (t d) -> p t d", t=MT), ACT.Copy).then_inc(vt_evac, 1)
            act.wait_ge(kv_stored, 32)
            rnorm(r_mix, (td, tb), 1)
            act.activation(mem_k_hi[:], mem_k, ACT.Copy).then_inc(mem_hi, 1)

            with act.Fori(0, BLOCKS, 1) as b:
                g = g_blk(b, O_GATE)
                w_high(g)
                w_high(g.at(1))
                act.dma_start(m_dec[:], one(st_m[bass.ds(b, 1)])).then_inc(mdec_loaded, 16)
                act.dma_start(cv_in[:].rearrange("p a b c -> p (a b c)"),
                              one(st_conv[bass.ds(b, 1)])).then_inc(cvin_loaded, 16)
                read_out(act, g)
                act.activation(gi, gi, ACT.Identity, bias=col(C_GI)).then_inc(gate_i, 1)
                read_out(act, g.at(1))
                st = Steps(act, a_gate, b * 3, "a_gate", 3)
                st(act.activation(gz, gz, ACT.Identity, bias=col(C_GF)))
                st.settle()
                st(act.activation(gt1, gz, ACT.Abs))
                st.settle()
                st(act.activation(gt1, gt1, ACT.Exp, scale=-1.0))
                st.settle()
                act.activation(gt1, gt1, ACT.Ln, bias=1.0).then_inc(ls_done, 1)
                st.end()
                w_high(g_blk(b, O_HEAD))
                act.wait_ge(rows_pre, b + 1)
                act.activation(rows[:, W:2 * W + DEC], rows[:, W:2 * W + DEC], ACT.Exp)
                act.activation(rows[:, 2 * W + DEC:], rows[:, 2 * W + DEC:], ACT.Exp, scale=-1.0).then_inc(rows_exp, 1)
                act.wait_ge(rows_exp, b + 1)
                act.dma_start(rows_d, rows[0:P:32, :]).then_inc(rows_stored, 16)
                act.dma_start(one(o_sm[bass.ds(b, 1)]), m_deco[:]).then_inc(m_stored, 16)
                with act.Fori(0, 2, 1) as j:
                    for u in range(2):
                        h = j * 2 + u
                        hd = b * 4 + j * 2 + u
                        g = g_head(b, j, u)
                        w_high(g.at(1))
                        act.wait_ge(rows_stored, b * 16 + 16)
                        act.wait_ge(bc_used, hd + 1)
                        act.dma_start(bc, rows_d[bass.ds(h, 1), :].to_broadcast([P, 3 * W + DEC])).then_inc(bc_loaded, 16)
                        act.wait_ge(y_stored, b * 64 + 64)
                        act.dma_start(x[:, bass.ds(h * 2, 2), :], x_blk[bass.ds(b * KT + h * 2, 2)].rearrange("k p c -> p k c")).then_inc(x_loaded, 16)
                        read_out(act, g.at(0))
                        act.activation(qf, qf, ACT.Identity, bias=dyn(C_BIN + u * 7, j * 14)).then_inc(bias_done, 1)
                        act.wait_ge(st_stored, hd * 32 + 32)
                        act.dma_start(ds_dec[:, :, 0:P], one(st_c[bass.ds(hd, 1)]).rearrange("p (s c) -> p s c", s=DEC)).then_inc(c_loaded, 16)
                        act.dma_start(n_dec, one(st_n[bass.ds(hd, 1)])).then_inc(n_loaded, 16)
                        read_out(act, g.at(1))
                        act.activation(kf, kf, ACT.Identity, scale=KSCALE, bias=dyn(C_BK + u, j * 2)).then_inc(bias_done, 1)
                        w_high(g.at(2))
                        read_out(act, g.at(2))
                        act.activation(vf, vf, ACT.Identity, bias=dyn(C_BIN + u * 7 + 2, j * 14)).then_inc(bias_done, 1)
                        act.wait_ge(acol_t, hd + 1)
                        act.activation(a_col.rearrange("p c h -> p (c h)"),
                                       td[:, 0:CH * HEADS], ACT.Copy).then_inc(acol_done, 1)
                        act.wait_ge(acol_done, hd + 1)
                        act.wait_ge(e_pre, hd + 1)
                        for c in range(CH):
                            act.activation(emat[:, c * P:(c + 1) * P], emat[:, c * P:(c + 1) * P], ACT.Exp,
                                           bias=a_col[:, c, bass.ds(h, 1)]).then_inc(e_done, 1)

                        def ktv_evac(c):
                            act.wait_ge(t_done, hd * CH + (c + 1))
                            if c >= 2:
                                act.wait_ge(n_done, hd * CH + (c - 1))
                            act.activation(ktv[:, c % 2, 0:2 * P], ta[:, c % 2, 0:2 * P], ACT.Copy).then_inc(ktv_done, 1)

                        def nd(c):
                            act.wait_ge(n_done, hd * CH + (c + 1))
                            act.activation(numden[:, :, c * P:(c + 1) * P],
                                           tb[:, 0:2 * P].rearrange("p (a c) -> p a c", a=2), ACT.Copy).then_inc(nd_evac, 1)

                        def lsg(i, *args, **kw):
                            if i:
                                act.wait_ge(a_sig, hd * 3 + i)
                            act.activation(hsq, *args, **kw).then_inc(a_sig, 1)

                        ktv_evac(0)
                        w_high(g.at(3))
                        ktv_evac(1)
                        read_out(act, g.at(3))
                        lsg(0, of, ACT.Abs, bias=dyn(C_BIN + u * 7 + 3, j * 14))
                        nd(0)
                        lsg(1, hsq, ACT.Exp, scale=-1.0)
                        ktv_evac(2)
                        w_high(g.at(4))
                        nd(1)
                        ktv_evac(3)
                        lsg(2, hsq, ACT.Ln, bias=1.0)
                        read_out(act, g.at(4))
                        act.activation(cgc, cgc, ACT.Identity, bias=dyn(C_BIN + u * 7 + 4, j * 14)).then_inc(conv_bias, 1)
                        nd(2)
                        act.wait_ge(td_done, hd + 1)
                        act.activation(dk[0:1, :, 0:2 * P], ta[0:1, 0, :].rearrange("p (s c) -> p s c", s=DEC),
                                       ACT.Copy).then_inc(dk_done, 1)
                        act.wait_ge(sig_pre, hd + 1)
                        act.activation(of, of, ACT.Exp).then_inc(sig_done, 1)
                        w_high(g.at(5))
                        nd(3)
                        act.wait_ge(h_done, hd * 4 + 1)
                        act.activation(hsq[:, 0:2 * P], hraw[:, 0:2 * P], ACT.Square).then_inc(hsq_done, 1)
                        act.wait_ge(dn_done, hd + 1)
                        act.activation(numden[:, :, TOK:W], tb[:, 0:2 * DEC].rearrange("p (a c) -> p a c", a=2),
                                       ACT.Copy).then_inc(dnd_evac, 1)
                        act.wait_ge(h_done, hd * 4 + 4)
                        act.activation(hsq[:, 2 * P:W], hraw[:, 2 * P:W], ACT.Square).then_inc(hsq_done, 1)
                        w_high(g.at(6))
                        act.wait_ge(hn_done, hd + 1)
                        for bank, (c, wd) in zip((td, tb), GROUPS):
                            a = act.activation(hr[:, c:c + wd], bank[:, 0:wd], ACT.Ln, scale=1.0 / P, bias=col(C_EPS))
                        a.then_inc(a_head, 1)
                        act.wait_ge(a_head, hd + 1)
                        act.activation(hr, hr, ACT.Exp, scale=-0.5).then_inc(hr_done, 1)
                        act.wait_ge(yh_done, hd + 1)
                        act.activation(tile(act_hi, h + 4), hraw, ACT.Copy).then_inc(y_hi, 1)
                        act.wait_ge(yc_done, hd + 1)
                        act.activation(tile(act_hi, h), yc, ACT.Copy).then_inc(y_hi, 1)
                        w_high(g.at(7))
                        act.dma_start(one(o_sc[bass.ds(hd, 1)]).rearrange("p (s c) -> p s c", s=DEC), ds_dec[:, :, 0:P]).then_inc(st_stored, 16)
                        act.dma_start(one(o_sn[bass.ds(hd, 1)]), n_dec).then_inc(st_stored, 16)
                def res_tile(g, e, use, gain):
                    for n, (c, wd) in enumerate(GROUPS):
                        act.wait_ge(res_acc, b * 51 + e * 2 + (use * 17 + n + 1))
                        act.wait_ge(evacuated, g.twice + (n + 5))
                        act.activation(sq_res[:, c:c + wd], cols(x, e, n), ACT.Square).then_inc(res_sq, 1)
                        if gain is not None:
                            act.activation(cols(xn_hi, e, n), cols(x, e, n), ACT.Copy, scale=dyn(gain, e)).then_inc(res_hi, 1)

                def cache(e):
                    act.dma_start(big[:, bass.ds(e * 1024, 1024)], one(kvc_d[bass.ds(b * 8 + e, 1)])).then_inc(cache_loaded, 16)

                act.wait_ge(y_lo, b * 8 + 8)
                act.dma_start(one(o_sconv[bass.ds(b, 1)]), cv_out[:].rearrange("p a b c -> p (a b c)")).then_inc(cv_stored, 16)
                res_tile(g_blk(b, O_OUT), 0, 0, C_GCROSS)
                with act.Fori(0, KT // 2 - 1, 1) as j:
                    for i in range(2):
                        g = g_blk(b, O_OUT, j).at(i + 1)
                        w_high(g)
                        res_tile(g, j * 2 + (i + 1), 0, C_GCROSS)
                        cache(j * 2 + i)
                g = g_blk(b, O_OUT, KT // 2 - 1).at(1)
                res_tile(g, KT - 1, 0, C_GCROSS)
                w_high(g)
                act.wait_ge(st_stored, b * (32 * HEADS) + 32 * (HEADS + 1))
                def exps(h, ts):
                    for t in ts:
                        act.wait_ge(mx_done, b * 8 + (h * 2 + t // 2 + 1))
                        act.activation(prob[:, t, :], ta[:, t // 2, (t % 2) * 256:(t % 2) * 256 + 256], ACT.Exp,
                                       scale=XSCALE, bias=mx[:, t, 1:2], accum_out=mx[:, t, 2:3]).then_inc(exp_done, 1)

                def pt(h, ts):
                    for t in ts:
                        act.wait_ge(pt_done, b * 16 + (h * 4 + t + 1))
                        act.activation(prob_t[:, :, t * P:(t + 1) * P],
                                       (tb, td)[t % 2][:, 0:256].rearrange("p (m c) -> p m c", m=MT),
                                       ACT.Copy).then_inc(pt_evac, 1)

                def out_high(h):
                    for dt, bank in enumerate((tb, td)):
                        act.wait_ge(pv_done, b * 8 + (h * 2 + dt + 1))
                        act.activation(act_hi[:, 2 * h + dt, 0:TOK], bank[:, :], ACT.Copy).then_inc(o_hi, 1)

                def q_high(m):
                    read_out(act, g_blk(b, O_XQ).at(m))
                    act.activation(act_hi[:, m, 0:TOK], q_att[:, (m // 2) % 2, m % 2, 0:TOK], ACT.Copy).then_inc(q_hi_done, 1)

                w_high(g_blk(b, O_XQ))
                rnorm(r_res, (ta[:, 0, :], ta[:, 1, :]), b * 4 + 2)
                cache(6)
                w_high(g_blk(b, O_XQ).at(1))
                cache(7)
                q_high(0)
                q_high(1)
                for h in range(HEADS - 1):
                    exps(h, range(4))
                    w_high(g_blk(b, O_XQ).at(2 * h + 2))
                    pt(h, (0, 1))
                    q_high(2 * h + 2)
                    pt(h, (2, 3))
                    w_high(g_blk(b, O_XQ).at(2 * h + 3))
                    q_high(2 * h + 3)
                    out_high(h)
                h = HEADS - 1
                exps(h, range(4))
                pt(h, (0,))
                act.wait_ge(dmx_done, b + 1)
                act.activation(pd[0:8, :], gb[0:8, 0, 0:NMEM], ACT.Exp, scale=XSCALE, bias=dmx[0:8, 1:2],
                               accum_out=dmx[0:8, 2:3]).then_inc(dexp_done, 1)
                pt(h, (1, 2, 3))
                act.wait_ge(dpt_done, b + 1)
                for i in range(DEC):
                    a = act.activation(pz[:, :, i, i * 4:i * 4 + 4],
                                       gb[:, 2, 0:16].rearrange("p (t c) -> p t c", t=MT)[:, :, i * 4:i * 4 + 4], ACT.Copy)
                a.then_inc(dpt_evac, 1)
                out_high(h)
                for half in range(2):
                    act.wait_ge(dpv_done, b * 2 + (half + 1))
                    act.activation(o_sb[0:8, half * 512:(half + 1) * 512], ta[0:8, half, :], ACT.Copy).then_inc(do_evac, 1)
                act.wait_ge(dot_done, b + 1)
                for cols_out, c in dec_cols:
                    a = act.activation(act_hi[cols_out], gb[:, 3, c], ACT.Copy)
                a.then_inc(do_hi, 1)
                with act.Fori(0, KT // 2, 1) as j:
                    for i in range(2):
                        g = g_blk(b, O_XO, j).at(i)
                        e = j * 2 + i
                        act.dma_start(tile(x_next, e), one(x_blk[bass.ds(b * KT + e + KT, 1)])).then_inc(xnext_loaded, 16)
                        res_tile(g, e, 1, C_GFFN)
                        w_high(g)
                rnorm(r_res, (ta[:, 0, :], ta[:, 1, :]), b * 4 + 3)
                fo = 0
                for gr, size in enumerate(FFG):
                    with act.Fori(0, size, 1) as f:
                        g = g_blk(b, O_FF[gr], f)
                        fi = b * 44 + f * 2 + 2 * fo

                        def e_part(n):
                            c, wd = GROUPS[n]
                            act.wait_ge(evacuated, g.twice + (n + 5))
                            act.activation(et[:, c:c + wd], gt[:, c:c + wd], ACT.Exp, scale=-1.0).then_inc(e_ffn, 1)

                        def h_part(n):
                            c, wd = GROUPS[n]
                            act.wait_ge(h_ffn, fi + (n + 1))
                            act.activation(cols(act_hi, f, n), ht[:, c:c + wd], ACT.Copy).then_inc(hid_hi, 1)

                        e_part(0)
                        w_high(g)
                        e_part(1)
                        h_part(0)
                        w_high(g.at(1))
                        h_part(1)
                    fo += size
                    if gr == len(FFG) - 1:
                        act.wait_ge(xnext_loaded, b * 128 + 144)
                    first_down = g_blk(b, O_FF[gr] + 2 * size)

                    def next_norm(e):
                        act.wait_ge(mix_acc, b * 9 + e + 19)
                        act.activation(tile(xn_hi, e), tile(x_next, e), ACT.Copy, scale=dyn(C_GMIX, e)).then_inc(mix_hi, 1)
                        act.activation(sq_mix[:], tile(x_next, e), ACT.Square).then_inc(mix_sq, 1)

                    if gr < len(FFG) - 1:
                        with act.Fori(0, KT // 2, 1) as j:
                            for i in range(2):
                                w_high(g_blk(b, O_FF[gr] + 2 * size, j).at(i))
                    else:
                        next_norm(0)
                        with act.Fori(0, KT // 2 - 1, 1) as j:
                            for i in range(2):
                                g = g_blk(b, O_FF[gr] + 2 * size, j).at(i)
                                w_high(g)
                                res_tile(g, j * 2 + i, 2, None)
                                next_norm(j * 2 + i + 1)
                        w_high(first_down.at(KT - 2))
                        res_tile(first_down.at(KT - 2), KT - 2, 2, None)
                        next_norm(KT - 1)
                        res_tile(first_down.at(KT - 1), KT - 1, 2, None)
                        w_high(first_down.at(KT - 1))
                act.wait_ge(ssq_done, b * 4 + 6)
                rnorm(r_res, (ta[:, 0, :], ta[:, 1, :]), b * 4 + 4)
                act.wait_ge(r_done, b * 4 + 5)
                rnorm(r_mix, (td, tb), b * 4 + 5)
                for k in range(0, KT, 2):
                    act.wait_ge(y_ready, b * 8 + (k + 2))
                    act.dma_start(y[bass.ds(b * KT + k, 2)].rearrange("k p c -> p k c"), x[:, k:k + 2, :]).then_inc(y_stored, 16)
            act.dma_start(o_pconv, carry[:].rearrange("p a b -> p (a b)")).then_inc(out_stored, 16)
            act.dma_start(o_pc, state[:].rearrange("p a b -> p (a b)")).then_inc(out_stored, 16)
            act.dma_start(o_pm, m_st[:]).then_inc(out_stored, 16)
            act.wait_ge(out_stored, 48)
            act.wait_ge(y_stored, 64 * (BLOCKS + 1))
            act.wait_ge(m_stored, 16 * (BLOCKS + 1))
            act.wait_ge(cv_stored, 16 * (BLOCKS + 1))
            act.wait_ge(st_stored, 32 * (BLOCKS * HEADS + 1))
            for i in range(2):
                act.wait_ge(w_loaded[i], 8 * G_ALL + 16)

        @block.vector
        def _(v):
            def col(c):
                return cst[:, c:c + 1]

            def dyn(c, e):
                return cst[:, bass.ds(e + c, 1)]

            v.sem_inc(evacuated, 4)
            for s, n in ((hr_done, 1), (o_lo, 1), (bc_used, 1), (y_stored, 64), (m_stored, 16), (cv_stored, 16),
                         (st_stored, 32)):
                v.sem_inc(s, n)
            v.memset(acc_mix[:], 0.0).then_inc(mix_acc, 1)
            for t, val in ((state[:], 0.0), (carry[:], 0.0), (m_st[:], 0.0)):
                v.memset(t, val).then_inc(set_up, 1)
            v.wait_ge(cst_loaded, 16)
            nbias = [(C_BK + h, C_BIN + 7 * h + 1, KSCALE) for h in range(HEADS)]
            for dst, src, f in nbias:
                v.tensor_scalar(col(dst), col(src), f, None, ALU.mult).then_inc(set_up, 1)
            v.wait_ge(set_up, 3 + len(nbias))

            def prep(src, gain, hi, lo, hi_sem, hi_count, lo_sem):
                v.wait_ge(hi_sem, hi_count)
                v.scalar_tensor_tensor(out=lo, in0=src, scalar=gain, in1=hi, op0=ALU.mult,
                                       op1=ALU.subtract).then_inc(lo_sem, 1)

            def add_sq(acc, sq, sq_sem, count, acc_sem, acc_count, width=W):
                v.wait_ge(sq_sem, count)
                v.wait_ge(acc_sem, acc_count)
                v.tensor_tensor(acc[:, 0:width], acc[:, 0:width], sq[:, 0:width], ALU.add).then_inc(acc_sem, 1)

            def w_low(g, ahead):
                v.wait_ge(w_hi_done, g.half * 2 + (g.k + ahead))
                v.tensor_tensor(w_lo[:, g.k, :], w_raw[:, g.k, :], w_hi[:, g.k, :].bitcast(F32),
                                ALU.subtract).then_inc(w_lo_done, 1)

            v.wait_ge(memx_loaded, 16)
            for k in range(KT):
                prep(memx[:, k, :], col(C_GMEM + k), act_hi[:, k, 0:NMEM].bitcast(F32), act_lo[:, k, 0:NMEM],
                     mix_hi, k + 1, mix_lo)
                add_sq(acc_mix, sq_mix, mix_sq, k + 1, mix_acc, k + 1, NMEM)
                if k < 2:
                    w_low(Gemm(0, k), 1)
            v.wait_ge(r_done, 1)
            v.memset(acc_mix[:], 0.0).then_inc(mix_acc, 1)
            v.wait_ge(xnext_loaded, 16)
            for base, dst in ((0, mem_k), (KT // 2, vfeat)):
                with v.Fori(0, KT // 2, 1) as j:
                    for i in range(2):
                        g = Gemm(j + base, i)
                        v.wait_ge(group_done, g.twice + 2)
                        v.tensor_tensor(tile(dst, j * 2 + i), gb[:, 2 * i, 0:NMEM], r_mix[:, 0:NMEM],
                                        ALU.mult).then_inc(evacuated, 2)
                        w_low(g, 3)
                    e = j + base
                    prep(tile(x_next, e), dyn(C_GMIX, e), tile(xn_hi, e).bitcast(F32), tile(xn_lo, e),
                         mix_hi, e + 9, mix_lo)
                    add_sq(acc_mix, sq_mix, mix_sq, e + 9, mix_acc, e + 10)

            def evac_one(g, n, f):
                v.wait_ge(group_done, g.twice + (n + 1))
                c, wd = GROUPS[n]
                f(slice(c, c + wd), gb[:, 2 * g.slot + n, 0:wd]).then_inc(evacuated, 1)

            def evac(g, f):
                for n in range(2):
                    evac_one(g, n, f)

            def scaled(dst, r):
                return lambda c, ps: v.tensor_tensor(dst[:, c], ps, r[:, c], ALU.mult)

            v.wait_ge(mats_loaded, 16)
            v.wait_ge(mem_hi, 1)
            v.tensor_tensor(mem_k_lo[:], mem_k, mem_k_hi[:].bitcast(F32), ALU.subtract).then_inc(set_up, 1)
            with v.Fori(0, BLOCKS, 1) as b:
                st = Steps(v, v_gate, b * STEPS["v_gate"], "v_gate", STEPS["v_gate"])
                st(v.memset(ktv[:, :, 2 * P:2 * P + 1], 1.0))
                st(v.memset(d0, 0.0))
                st(v.memset(dk[0:1, :, 2 * P:2 * P + 1], 1.0))
                g = g_blk(b, O_GATE)
                v.wait_ge(r_done, b * 4 + 2)
                v.memset(acc_mix[:], 0.0).then_inc(mix_acc, 1)
                evac(g, scaled(gi, r_mix))
                evac(g.at(1), scaled(gz, r_mix))
                v.wait_ge(ls_done, b + 1)
                st(v.scalar_tensor_tensor(out=gt1, in0=gz, scalar=0.0, in1=gt1, op0=ALU.min, op1=ALU.subtract))
                st.settle()
                st(v.tensor_tensor_scan(brow, reset, gt1, 0.0, ALU.mult, ALU.add))
                st.settle()
                v.wait_ge(gate_i, b + 1)
                st(v.tensor_tensor(a_row[:], gi, brow, ALU.subtract))
                st(v.tensor_copy(d0[:, P:TOK:P], brow[:, P - 1:TOK - P:P]))
                st.settle()
                v.wait_ge(mdec_loaded, b * 16 + 16)
                v.wait_ge(m_stored, b * 16 + 16)
                v.wait_ge(cv_stored, b * 16 + 16)
                st(v.tensor_tensor_scan(rows[:, 0:TOK], d0, a_row[:, 0:TOK], m_st[:, 0:1], ALU.add, ALU.max))
                st(v.tensor_tensor(rows[:, TOK:W], m_dec[:], a_row[:, TOK:W], ALU.max))
                st.settle()
                st(v.tensor_tensor(m_st[:, 1:CH + 1], brow[:, P - 1:TOK:P], rows[:, P - 1:TOK:P], ALU.add))
                st(v.tensor_tensor(rows[:, 2 * W + DEC:], brow, rows[:, 0:W], ALU.add))
                st(v.tensor_tensor(rows[:, W + TOK:2 * W], m_dec[:], rows[:, TOK:W], ALU.subtract))
                st(v.tensor_tensor(rows[:, 2 * W:2 * W + DEC], a_row[:, TOK:W], rows[:, TOK:W], ALU.subtract))
                st(v.tensor_tensor(m_deco[:], brow[:, TOK:W], rows[:, TOK:W], ALU.add))
                st.settle()
                v.tensor_tensor(rows[:, W:W + TOK].rearrange("p (c l) -> p c l", c=CH),
                                m_st[:, 0:CH].rearrange("p (c o) -> p c o", o=1).to_broadcast([P, CH, P]),
                                rows[:, 0:TOK].rearrange("p (c l) -> p c l", c=CH), ALU.subtract).then_inc(rows_pre, 1)
                v.wait_ge(rows_pre, b + 1)
                st(v.tensor_copy(m_st[:, 0:1], m_st[:, CH:CH + 1]))
                st.end()
                with v.Fori(0, 2, 1) as j:
                    for u in range(2):
                        h = j * 2 + u
                        hd = b * 4 + j * 2 + u
                        g = g_head(b, j, u)
                        per = STEPS["v_head"]
                        st = Steps(v, v_head, hd * per, "v_head", per)
                        v.tensor_copy(ws, tile(state, h)).then_inc(state_done, 1)
                        evac(g, scaled(qf, r_mix))
                        evac(g.at(1), scaled(kf, r_mix))
                        v.wait_ge(bc_loaded, hd * 16 + 16)
                        v.tensor_tensor(emat.rearrange("p (c l) -> p c l", c=CH),
                                        maskneg.rearrange("p (o l) -> p o l", o=1).to_broadcast([P, CH, P]),
                                        bc[:, 0:TOK].rearrange("p (c l) -> p c l", c=CH), ALU.subtract).then_inc(e_pre, 1)
                        evac(g.at(2), scaled(vf, r_mix))
                        v.wait_ge(bias_done, hd * 3 + 1)
                        v.tensor_tensor(qg[:, 0:TOK], qf[:, 0:TOK], bc[:, W:W + TOK], ALU.mult).then_inc(qg_done, 1)
                        evac(g.at(3), scaled(of, r_mix))

                        def wv(c):
                            s = c % 2
                            last = emat[:, c * P + P - 1:c * P + P]
                            v.wait_ge(ktv_done, hd * CH + (c + 1))
                            v.wait_ge(e_done, hd * CH + (c + 1))
                            v.tensor_tensor(w_sb[:, s, :], ta[:, s, 2 * P:3 * P], emat[:, c * P:(c + 1) * P],
                                            ALU.mult).then_inc(w_done, 1)
                            v.tensor_scalar(vs_sb[:, s, :], ktv[:, s, P:P + V1], last, None, ALU.mult).then_inc(vs_done, 1)

                        def update(c):
                            decay = bc[:, W + c * P + P - 1:W + c * P + P]
                            v.wait_ge(nd_evac, hd * CH + (c + 1))
                            v.wait_ge(state_done, hd * 5 + (c + 1))
                            v.scalar_tensor_tensor(out=ws[:, 0:P], in0=ws[:, 0:P], scalar=decay, in1=tb[:, 2 * P:3 * P],
                                                   op0=ALU.mult, op1=ALU.add)
                            v.scalar_tensor_tensor(out=ws[:, P:2 * P], in0=ws[:, P:2 * P], scalar=decay,
                                                   in1=tb[:, 3 * P:3 * P + 1].to_broadcast([P, P]),
                                                   op0=ALU.mult, op1=ALU.add).then_inc(state_done, 1)

                        def h_cols(c0, c1):
                            num, den = numden[:, 0, c0:c1], numden[:, 1, c0:c1]
                            st(v.scalar_tensor_tensor(out=den, in0=den, scalar=-1.0, in1=den, op0=ALU.mult, op1=ALU.max))
                            st.settle()
                            st(v.tensor_tensor(den, den, bc[:, 2 * W + DEC + c0:2 * W + DEC + c1], ALU.max))
                            st.settle()
                            st(v.reciprocal(den, den))
                            st.settle()
                            v.tensor_tensor(hraw[:, c0:c1], num, den, ALU.mult).then_inc(h_done, 1)

                        wv(0)
                        wv(1)
                        evac_one(g.at(4), 0, scaled(cgc, r_mix))
                        update(0)
                        wv(2)
                        evac_one(g.at(4), 1, scaled(cgc, r_mix))
                        update(1)
                        wv(3)
                        h_cols(0, 2 * P)
                        v.wait_ge(a_sig, hd * 3 + 1)
                        st(v.tensor_scalar(of, of, dyn(C_BIN + u * 7 + 3, j * 14), 0.0, ALU.add, ALU.min))
                        evac_one(g.at(5), 0, scaled(chc, r_mix))
                        update(2)
                        v.wait_ge(dk_done, hd + 1)
                        for i in range(DEC):
                            a = v.tensor_scalar(dvs[0:1, i, :], dk[0:1, i, P:P + V1], bc[0:1, 2 * W + i:2 * W + i + 1],
                                                None, ALU.mult)
                        a.then_inc(dvs_done, 1)
                        v.wait_ge(a_sig, hd * 3 + 3)
                        st.settle()
                        v.tensor_tensor(of, of, hsq, ALU.subtract).then_inc(sig_pre, 1)
                        v.wait_ge(c_loaded, hd * 16 + 16)
                        v.wait_ge(n_loaded, hd * 16 + 16)
                        for i in range(DEC):
                            st(v.tensor_copy(ds_dec[:, i, P:2 * P], n_dec[:, i:i + 1].to_broadcast([P, P])))
                        h_cols(2 * P, 3 * P)
                        evac_one(g.at(5), 1, scaled(chc, r_mix))
                        update(3)
                        v.wait_ge(state_done, hd * 5 + 5)
                        st.settle()
                        v.wait_ge(dupd_done, hd + 1)
                        for i in range(DEC):
                            decay = bc[:, W + TOK + i:W + TOK + i + 1]
                            st(v.scalar_tensor_tensor(out=ds_dec[:, i, 0:P], in0=ds_dec[:, i, 0:P], scalar=decay,
                                                      in1=td[:, i * 256:i * 256 + P], op0=ALU.mult, op1=ALU.add))
                            st(v.scalar_tensor_tensor(out=ds_dec[:, i, P:2 * P], in0=ds_dec[:, i, P:2 * P], scalar=decay,
                                                      in1=td[:, i * 256 + P:i * 256 + V1].to_broadcast([P, P]),
                                                      op0=ALU.mult, op1=ALU.add))
                        st.settle()
                        v.tensor_copy(n_dec, ds_dec[:, :, P]).then_inc(dstate_done, 1)
                        v.wait_ge(nd_evac, hd * CH + 4)
                        h_cols(3 * P, TOK)
                        st(v.tensor_copy(tile(state, h), ws))
                        v.wait_ge(dnd_evac, hd + 1)
                        h_cols(TOK, W)
                        v.wait_ge(h_done, hd * 4 + 4)
                        v.sem_inc(bc_used, 1)
                        st(v.tensor_copy(ub[:, 0:2], tile(carry, h)))
                        v.wait_ge(conv_bias, hd + 1)
                        read_out(v, g.at(5))
                        st(v.scalar_tensor_tensor(out=ub[:, 2:W + 2], in0=chc, scalar=dyn(C_BIN + u * 7 + 5, j * 14),
                                                  in1=cgc, op0=ALU.add, op1=ALU.mult))
                        evac_one(g.at(6), 0, scaled(cgb, r_mix))
                        st.settle()
                        v.wait_ge(cvin_loaded, b * 16 + 16)
                        tap = [dyn(C_CW + 3 * u + i, j * 6) for i in range(3)]
                        cin = cv_in[:, bass.ds(h, 1), :, :].rearrange("p o r i -> p (o r) i")
                        cout = cv_out[:, bass.ds(h, 1), :, :].rearrange("p o r i -> p (o r) i")
                        st(v.tensor_scalar(yc[:, 0:TOK], ub[:, 0:TOK], tap[0], None, ALU.mult))
                        st(v.tensor_scalar(yc[:, TOK:W], cin[:, 0, :], tap[0], None, ALU.mult))
                        st(v.tensor_copy(cout[:, 0, :], cin[:, 1, :]))
                        st(v.tensor_copy(cout[:, 1, :], ub[:, TOK + 2:W + 2]))
                        st(v.tensor_copy(tile(carry, h), ub[:, TOK:TOK + 2]))
                        st.settle()
                        st(v.scalar_tensor_tensor(out=yc[:, 0:TOK], in0=ub[:, 1:TOK + 1], scalar=tap[1],
                                                  in1=yc[:, 0:TOK], op0=ALU.mult, op1=ALU.add))
                        st(v.scalar_tensor_tensor(out=yc[:, TOK:W], in0=cin[:, 1, :], scalar=tap[1],
                                                  in1=yc[:, TOK:W], op0=ALU.mult, op1=ALU.add))
                        evac_one(g.at(6), 1, scaled(cgb, r_mix))
                        v.wait_ge(hr_done, hd + 2)
                        st(v.tensor_tensor(hraw, hraw, hr, ALU.mult))
                        st.settle()
                        st(v.scalar_tensor_tensor(out=yc, in0=ub[:, 2:W + 2], scalar=tap[2], in1=yc,
                                                  op0=ALU.mult, op1=ALU.add))
                        v.wait_ge(sig_done, hd + 1)
                        v.scalar_tensor_tensor(out=hraw, in0=hraw, scalar=dyn(C_GMH + u, j * 2), in1=of,
                                               op0=ALU.mult, op1=ALU.mult).then_inc(yh_done, 1)
                        st.settle()
                        read_out(v, g.at(6))
                        v.scalar_tensor_tensor(out=yc, in0=cgb, scalar=dyn(C_BIN + u * 7 + 6, j * 14), in1=yc,
                                               op0=ALU.add, op1=ALU.mult).then_inc(yc_done, 1)
                        v.wait_ge(y_hi, hd * 2 + 1)
                        v.tensor_tensor(tile(act_lo, h + 4), hraw, tile(act_hi, h + 4).bitcast(F32),
                                        ALU.subtract).then_inc(y_lo, 1)
                        v.wait_ge(y_hi, hd * 2 + 2)
                        v.tensor_tensor(tile(act_lo, h), yc, tile(act_hi, h).bitcast(F32), ALU.subtract).then_inc(y_lo, 1)
                        st.end()

                def add_x(e):
                    return lambda c, ps: v.tensor_tensor(x_cols(e, c), x_cols(e, c), ps, ALU.add)

                def x_cols(e, c):
                    return x[:, bass.ds(e, 1), c].rearrange("p o c -> p (o c)")

                def res_tile(g, e, use, gain, ahead=False):
                    if ahead:
                        evac(g, add_x(e))
                    for n, (c, wd) in enumerate(GROUPS):
                        if not ahead:
                            evac_one(g, n, add_x(e))
                        v.wait_ge(evacuated, g.twice + (n + 5))
                        v.wait_ge(res_sq, b * 48 + e * 2 + (use * 16 + n + 1))
                        v.wait_ge(res_acc, b * 51 + e * 2 + (use * 17 + n + 1))
                        v.tensor_tensor(acc_res[:, c:c + wd], acc_res[:, c:c + wd], sq_res[:, c:c + wd],
                                        ALU.add).then_inc(res_acc, 1)
                        if gain is not None:
                            v.wait_ge(res_hi, b * 32 + e * 2 + (use * 16 + n + 1))
                            v.scalar_tensor_tensor(out=cols(xn_lo, e, n), in0=cols(x, e, n), scalar=dyn(gain, e),
                                                   in1=cols(xn_hi, e, n).bitcast(F32), op0=ALU.mult,
                                                   op1=ALU.subtract).then_inc(res_lo, 1)

                v.wait_ge(x_loaded, b * 64 + 64)
                v.memset(acc_res[:], 0.0).then_inc(res_acc, 1)
                with v.Fori(0, KT // 2, 1) as j:
                    for i in range(2):
                        res_tile(g_blk(b, O_OUT, j).at(i), j * 2 + i, 0, C_GCROSS)
                v.wait_ge(r_done, b * 4 + 3)
                v.memset(acc_res[:], 0.0).then_inc(res_acc, 1)
                per = STEPS["v_att"]
                st = Steps(v, v_att, b * per, "v_att", per)

                def maxima(h):
                    for i in range(2):
                        v.wait_ge(s_done, b * 8 + (h * 2 + i + 1))
                        st(v.tensor_reduce(mx[:, 2 * i:2 * i + 2, 0], ta[:, i, :].rearrange("p (t m) -> p t m", t=2),
                                           AX.X, ALU.max))
                        st.settle()
                        v.tensor_scalar(mx[:, 2 * i:2 * i + 2, 1], mx[:, 2 * i:2 * i + 2, 0], -XSCALE, None,
                                        ALU.mult).then_inc(mx_done, 1)

                def normalise(h, ts):
                    for t in ts:
                        v.wait_ge(exp_done, b * 16 + (h * 4 + t + 1))
                        st(v.reciprocal(mx[:, t, 3:4], mx[:, t, 2:3]))
                        st.settle()
                        v.tensor_scalar(prob[:, t, :], prob[:, t, :], mx[:, t, 3:4], None, ALU.mult).then_inc(p_done, 1)

                def out_low(h):
                    for dt, bank in enumerate((tb, td)):
                        v.wait_ge(o_hi, b * 8 + (h * 2 + dt + 1))
                        v.tensor_tensor(act_lo[:, 2 * h + dt, 0:TOK], bank[:, :],
                                        act_hi[:, 2 * h + dt, 0:TOK].bitcast(F32), ALU.subtract).then_inc(o_lo, 1)

                def xq(m):
                    return g_blk(b, O_XQ).at(m)

                def q_low(m):
                    v.wait_ge(q_hi_done, b * 8 + (m + 1))
                    v.tensor_tensor(act_lo[:, m, 0:TOK], q_att[:, (m // 2) % 2, m % 2, 0:TOK],
                                    act_hi[:, m, 0:TOK].bitcast(F32), ALU.subtract).then_inc(q_lo_done, 1)

                def q_dec(h):
                    read_out(v, xq(2 * h + 1))
                    for dt in range(2):
                        c = h * 17 + dt * 8
                        q = v.tensor_copy(qz[:, c:c + 69:68], q_att[:, h % 2, dt, TOK:W])
                    q.then_inc(qd_done, 1)

                st(v.memset(qz, 0.0))
                st(v.memset(pz, 0.0))
                evac(xq(0), scaled(q_att[:, 0, 0, :], r_res))
                evac(xq(1), scaled(q_att[:, 0, 1, :], r_res))
                q_low(0)
                q_low(1)
                st.settle()
                q_dec(0)
                for h in range(HEADS - 1):
                    s = (h + 1) % 2
                    evac_one(xq(2 * h + 2), 0, scaled(q_att[:, s, 0, :], r_res))
                    maxima(h)
                    normalise(h, range(4))
                    evac_one(xq(2 * h + 2), 1, scaled(q_att[:, s, 0, :], r_res))
                    evac_one(xq(2 * h + 3), 0, scaled(q_att[:, s, 1, :], r_res))
                    q_low(2 * h + 2)
                    evac_one(xq(2 * h + 3), 1, scaled(q_att[:, s, 1, :], r_res))
                    q_low(2 * h + 3)
                    q_dec(h + 1)
                    out_low(h)
                h = HEADS - 1
                maxima(h)
                normalise(h, range(4))
                v.wait_ge(ds_done, b + 1)
                st(v.tensor_reduce(dmx[0:8, 0:1], gb[0:8, 0, 0:NMEM], AX.X, ALU.max))
                st.settle()
                v.tensor_scalar(dmx[0:8, 1:2], dmx[0:8, 0:1], -XSCALE, None, ALU.mult).then_inc(dmx_done, 1)
                v.wait_ge(dexp_done, b + 1)
                st(v.reciprocal(dmx[0:8, 3:4], dmx[0:8, 2:3]))
                st.settle()
                v.tensor_scalar(pd[0:8, :], pd[0:8, :], dmx[0:8, 3:4], None, ALU.mult).then_inc(dp_done, 1)
                out_low(h)
                st.end()
                v.wait_ge(do_hi, b + 1)
                for cols_out, c in dec_cols:
                    a = v.tensor_tensor(act_lo[cols_out], gb[:, 3, c], act_hi[cols_out].bitcast(F32), ALU.subtract)
                a.then_inc(do_lo, 1)
                with v.Fori(0, KT // 2, 1) as j:
                    for i in range(2):
                        res_tile(g_blk(b, O_XO, j).at(i), j * 2 + i, 1, C_GFFN)
                v.wait_ge(r_done, b * 4 + 4)
                v.memset(acc_res[:], 0.0).then_inc(res_acc, 1)
                fo = 0
                for gr, size in enumerate(FFG):
                    with v.Fori(0, size, 1) as f:
                        g = g_blk(b, O_FF[gr], f)
                        fi = b * 22 + f + fo
                        st = Steps(v, v_ffn, fi * 6, "v_ffn", 6)

                        def part(t, n):
                            c, wd = GROUPS[n]
                            return t[:, c:c + wd]

                        def silu_pre(n):
                            v.wait_ge(e_ffn, fi * 2 + (n + 1))
                            st(v.tensor_scalar(part(et, n), part(et, n), 1.0, None, ALU.add))
                            st.settle()
                            st(v.reciprocal(part(et, n), part(et, n)))

                        def silu(n):
                            st.settle()
                            st(v.tensor_tensor(part(gt, n), part(gt, n), part(et, n), ALU.mult))

                        def hidden(n):
                            v.wait_ge(evacuated, g.at(1).twice + (n + 5))
                            st.settle()
                            v.tensor_tensor(part(ht, n), part(gt, n), part(ut, n), ALU.mult).then_inc(h_ffn, 1)
                            v.wait_ge(hid_hi, fi * 2 + (n + 1))
                            v.tensor_tensor(cols(act_lo, f, n), part(ht, n), cols(act_hi, f, n).bitcast(F32),
                                            ALU.subtract).then_inc(hid_lo, 1)

                        evac_one(g, 0, scaled(gt, r_res))
                        silu_pre(0)
                        evac_one(g, 1, scaled(gt, r_res))
                        silu(0)
                        silu_pre(1)
                        silu(1)
                        evac_one(g.at(1), 0, scaled(ut, r_res))
                        hidden(0)
                        evac_one(g.at(1), 1, scaled(ut, r_res))
                        hidden(1)
                        st.end()
                    fo += size
                    first_down = g_blk(b, O_FF[gr] + 2 * size)

                    def next_norm(e):
                        prep(tile(x_next, e), dyn(C_GMIX, e), tile(xn_hi, e).bitcast(F32), tile(xn_lo, e),
                             mix_hi, b * 8 + e + 17, mix_lo)
                        add_sq(acc_mix, sq_mix, mix_sq, b * 8 + e + 17, mix_acc, b * 9 + e + 19)

                    if gr < len(FFG) - 1:
                        with v.Fori(0, KT // 2, 1) as j:
                            for i in range(2):
                                evac(g_blk(b, O_FF[gr] + 2 * size, j).at(i), add_x(j * 2 + i))
                    else:
                        next_norm(0)
                        with v.Fori(0, KT // 2 - 1, 1) as j:
                            for i in range(2):
                                res_tile(g_blk(b, O_FF[gr] + 2 * size, j).at(i), j * 2 + i, 2, None, ahead=True)
                                next_norm(j * 2 + i + 1)
                        res_tile(first_down.at(KT - 2), KT - 2, 2, None, ahead=True)
                        next_norm(KT - 1)
                        res_tile(first_down.at(KT - 1), KT - 1, 2, None)
                v.wait_ge(r_done, b * 4 + 5)
                for k in range(KT):
                    v.scalar_tensor_tensor(out=x[:, k, :], in0=x[:, k, :], scalar=col(C_GFIN + k), in1=r_res[:],
                                           op0=ALU.mult, op1=ALU.mult).then_inc(y_ready, 1)


def kernel(x_prompt, x_sample, mem_prompt, state_conv, state_mlstm_C, state_mlstm_n, state_mlstm_m,
           cache_mem_k, cache_mem_v, g_mix, w_in, b_in, conv_w, g_mh, w_out, g_cross, g_mem,
           w_xq, w_xkv, w_xo, g_ffn, w_gu, w_down, g_final):
    import concourse.bacc as bacc
    from concourse.bass_utils import run_bass_kernel_spmd

    f = np.float32
    A = np.ascontiguousarray

    def feat(a):
        return A(np.asarray(a).T.reshape(KT, P, -1).transpose(1, 0, 2))

    def chunk(w, c0, n=P):
        k = w.shape[0] // P
        out = np.zeros((P, KT, P), f)
        out[:, :k, :n] = w[:, c0:c0 + n].reshape(k, P, n).transpose(1, 0, 2)
        return out.reshape(P, KT * P)

    xp = feat(np.asarray(x_prompt)[0])
    xs = feat(np.asarray(x_sample)[:, 0])
    x_blk = np.zeros((BLOCKS + 1, KT, P, W), f)
    for b in range(BLOCKS):
        x_blk[b, :, :, :TOK] = xp[:, :, b * TOK:(b + 1) * TOK].transpose(1, 0, 2)
        x_blk[b, :, :, TOK:] = xs[:, :, b * DEC:(b + 1) * DEC].transpose(1, 0, 2)
    wi, bi = np.asarray(w_in)[0], np.asarray(b_in)[0]
    C2 = 512
    GO = 7 * C2
    gate_w, gate_b = [], []
    for part in range(2):
        t = np.zeros((D, P), f)
        t[:, ::32] = wi[:, GO + 4 * part:GO + 4 * part + 4]
        gate_w.append(chunk(t, 0))
        v = np.zeros(P, f)
        v[::32] = bi[GO + 4 * part:GO + 4 * part + 4]
        gate_b.append(v)
    order = [s * C2 for s in (3, 4, 5, 6, 1, 2, 0)]
    st = list(gate_w)
    for h in range(HEADS):
        st += [chunk(wi, o + h * P) for o in order]
    for w in (w_out, w_xq, w_xo):
        st += [chunk(np.asarray(w)[0], m * P) for m in range(KT)]
    gu, dn = np.asarray(w_gu)[0], np.asarray(w_down)[0]
    fo = 0
    for size in FFG:
        for i in range(fo, fo + size):
            st += [chunk(gu, i * P), chunk(gu, FF + i * P)]
        st += [chunk(dn[fo * P:(fo + size) * P], m * P) for m in range(KT)]
        fo += size
    w_st = np.stack(st)
    w_kv = np.stack([chunk(np.asarray(w_xkv)[0], m * P) for m in range(2 * KT)])
    cst = np.zeros((P, NCST), f)
    for h in range(HEADS):
        for s, o in enumerate(order):
            cst[:, C_BIN + 7 * h + s] = bi[o + h * P:o + (h + 1) * P]
        cst[:, C_CW + 3 * h:C_CW + 3 * h + 3] = np.asarray(conv_w)[0, :, h * P:(h + 1) * P].T
        cst[:, C_GMH + h] = np.asarray(g_mh)[0, h * P:(h + 1) * P]
    cst[:, C_GI], cst[:, C_GF] = gate_b
    for c, gg in ((C_GMIX, np.asarray(g_mix)[0]), (C_GCROSS, np.asarray(g_cross)[0]), (C_GMEM, np.asarray(g_mem)[0]),
                  (C_GFFN, np.asarray(g_ffn)[0]), (C_GFIN, np.asarray(g_final))):
        cst[:, c:c + KT] = gg.reshape(KT, P).T
    cst[:, C_EPS] = EPS
    idx = np.arange(P)
    mats = np.zeros((P, 3 * P + W), f)
    mats[:, 0:P] = np.eye(P)
    mats[:, P:2 * P] = 1
    mats[:, 2 * P:3 * P] = np.where(idx[:, None] > idx[None, :], MASKED, 0)
    mats[:, 3 * P:] = 1
    mats[:, 3 * P:3 * P + TOK:CHUNK] = 0
    mats[:, 3 * P + TOK:] = 0
    sc = np.asarray(state_conv)[0].reshape(BLOCKS, DEC, 2, HEADS, P)
    st_conv = A(sc.transpose(0, 4, 3, 2, 1)).reshape(BLOCKS, P, HEADS * 2 * DEC)
    c_ = np.asarray(state_mlstm_C)[0].reshape(BLOCKS, DEC, HEADS, P, P)
    st_c = A(c_.transpose(0, 2, 4, 1, 3)).reshape(BLOCKS * HEADS, P, DEC * P)
    n_ = np.asarray(state_mlstm_n)[0].reshape(BLOCKS, DEC, HEADS, P)
    st_n = A(n_.transpose(0, 2, 3, 1)).reshape(BLOCKS * HEADS, P, DEC)
    st_m = np.zeros((BLOCKS, P, DEC), f)
    st_m[:, ::32, :] = np.asarray(state_mlstm_m)[0].reshape(BLOCKS, DEC, HEADS).transpose(0, 2, 1)
    k_ = np.asarray(cache_mem_k)[0].reshape(BLOCKS, DEC, NMEM, HEADS, 2, P)
    kc = k_.transpose(0, 5, 1, 3, 4, 2).reshape(BLOCKS, P, 4, 1024)
    v_ = np.asarray(cache_mem_v)[0].reshape(BLOCKS, DEC, MT, P, D)
    vc = v_.transpose(0, 3, 1, 2, 4).reshape(BLOCKS, P, 4, 1024)
    kvc = A(np.concatenate([kc, vc], 2).transpose(0, 2, 1, 3)).reshape(BLOCKS * 8, P, 1024)

    ins = {"x_blk": x_blk.reshape(-1, P, W), "mem_x": feat(np.asarray(mem_prompt)[0]).reshape(P, -1),
           "w_kv": w_kv, "w_st": w_st, "cst_d": cst, "mats_d": mats, "st_conv": st_conv, "st_c": st_c,
           "st_n": st_n, "st_m": st_m, "kvc_d": kvc}
    outs = {"y": (BLOCKS * KT, P, W), "o_pconv": (P, HEADS * 2), "o_pc": (P, HEADS * 256), "o_pm": (P, CH + 1),
            "o_mk": (P, KT * NMEM), "o_mv": (P, KT * NMEM), "o_sconv": (BLOCKS, P, HEADS * 2 * DEC),
            "o_sc": (BLOCKS * HEADS, P, DEC * P), "o_sn": (BLOCKS * HEADS, P, DEC), "o_sm": (BLOCKS, P, DEC)}
    nc = bacc.Bacc("TRN2", target_bir_lowering=False, num_devices=1)
    aps = {n: nc.dram_tensor(n, a.shape, F32, kind="ExternalInput").ap() for n, a in ins.items()}
    aps.update({n: nc.dram_tensor(n, s, F32, kind="ExternalOutput").ap() for n, s in outs.items()})
    aps["rows_d"] = nc.dram_tensor("rows_d", (HEADS, 3 * W + DEC), F32, kind="Internal").ap()
    trunk(nc, **aps)
    res = run_bass_kernel_spmd(nc, [ins], core_ids=[0]).results[0]

    def tokens(a, n):
        return a.transpose(2, 1, 0).reshape(n, D)

    yb = res["y"].reshape(BLOCKS, KT, P, W).transpose(0, 2, 1, 3)
    y_p = np.concatenate([tokens(yb[b, :, :, :TOK], TOK) for b in range(BLOCKS)])[None]
    y_s = np.concatenate([tokens(yb[b, :, :, TOK:], DEC) for b in range(BLOCKS)])[:, None]
    p_conv = A(res["o_pconv"].reshape(P, HEADS, 2).transpose(2, 1, 0)).reshape(1, 1, 2, C2)
    pc = res["o_pc"].reshape(P, HEADS, 256)
    p_C = A(pc[:, :, 0:P].transpose(1, 2, 0))[None, None]
    p_n = A(pc[:, :, P].T)[None, None]
    p_m = A(res["o_pm"][::32, 0])[None, None]
    mk, mv = (tokens(res[n].reshape(P, KT, NMEM), NMEM).reshape(1, 1, NMEM, HEADS, 256) for n in ("o_mk", "o_mv"))
    s_conv = A(res["o_sconv"].reshape(BLOCKS, P, HEADS, 2, DEC).transpose(0, 4, 3, 2, 1)).reshape(1, NDEC, 2, C2)
    s_C = A(res["o_sc"].reshape(BLOCKS, HEADS, P, DEC, P).transpose(0, 3, 1, 4, 2)).reshape(1, NDEC, HEADS, P, P)
    s_n = A(res["o_sn"].reshape(BLOCKS, HEADS, P, DEC).transpose(0, 3, 1, 2)).reshape(1, NDEC, HEADS, P)
    s_m = A(res["o_sm"][:, ::32, :].transpose(0, 2, 1)).reshape(1, NDEC, HEADS)
    return (A(y_p), A(y_s), p_conv, p_C, p_n, p_m, A(mk), A(mv), s_conv, s_C, s_n, s_m)
```
